# Optimizing a Trainium2 kernel written in Bass

```python
import jax
import jax.numpy as jnp
from jax import lax
import numpy as np

D_MODEL = 1024
BATCH = 1
SEQ = 256
DEPTH = 2
DEC_BATCH = 1
DEC_SEQ = 64
PAST_LEN = 256

CHUNK = 64
D_MIX = D_MODEL
CONV_DIM = D_MIX // 2
CONV_W = 3
GLA_HEADS = 4
GLA_DV = D_MIX - CONV_DIM
GLA_HEAD_V = GLA_DV // GLA_HEADS
GLA_HEAD_K = GLA_HEAD_V // 2
GLA_QK = GLA_HEADS * GLA_HEAD_K
GATE_RANK = 16
GATE_TEMP = 16.0
D_FF = 3584
N_EXPERTS = 8
TOP_K = 2
N_DENSE = (DEPTH + 1) // 2
N_MOE = DEPTH // 2
ALPHA = (2 * DEPTH) ** 0.25
BETA = (8 * DEPTH) ** -0.25
LN_EPS = 1e-5
IN_COLS = 3 * CONV_DIM + 2 * GLA_QK + 2 * GLA_DV + GATE_RANK
IN_SPLITS = (CONV_DIM, 2 * CONV_DIM, 3 * CONV_DIM, 3 * CONV_DIM + GLA_QK, 3 * CONV_DIM + 2 * GLA_QK,
             3 * CONV_DIM + 2 * GLA_QK + GLA_DV, 3 * CONV_DIM + 2 * GLA_QK + 2 * GLA_DV)

kernel_name = "hymba_conv_gla_deepnorm_stream_step"

def _layer_norm(x, g, b):
    xf = x.astype(jnp.float32)
    mu = jnp.mean(xf, axis=-1, keepdims=True)
    var = jnp.mean(jnp.square(xf - mu), axis=-1, keepdims=True)
    y = (xf - mu) * lax.rsqrt(var + LN_EPS) * g.astype(jnp.float32) + b.astype(jnp.float32)
    return y.astype(x.dtype)

def _short_conv(u, buf, w):
    T = u.shape[1]
    u_ext = jnp.concatenate([buf.astype(u.dtype), u], axis=1)
    out = u_ext[:, 0:T] * w[0]
    for i in range(1, CONV_W):
        out = out + u_ext[:, i:i + T] * w[i]
    return out, u_ext[:, T:]

def _gla_chunked(q, k, v, log_a, s0):
    B, T, H, DK = q.shape
    DV = v.shape[-1]
    L = min(CHUNK, T)
    NC = T // L
    f32 = jnp.float32
    q = q.astype(f32).reshape(B, NC, L, H, DK)
    k = k.astype(f32).reshape(B, NC, L, H, DK)
    v = v.astype(f32).reshape(B, NC, L, H, DV)
    b = jnp.cumsum(log_a.astype(f32).reshape(B, NC, L, H, DK), axis=2)
    b_last = b[:, :, -1:]
    qg = q * jnp.exp(b)
    kg = k * jnp.exp(-b)
    kd = k * jnp.exp(b_last - b)
    causal = jnp.tril(jnp.ones((L, L), dtype=bool))
    scores = jnp.einsum('bnihk,bnjhk->bnhij', qg, kg)
    scores = jnp.where(causal, scores, 0.0)
    o_intra = jnp.einsum('bnhij,bnjhv->bnihv', scores, v)
    d_state = jnp.einsum('bnjhk,bnjhv->bnhkv', kd, v)
    decay = jnp.exp(b_last[:, :, 0])

    def step(s, inp):
        dec, ds = inp
        return dec[..., None] * s + ds, s

    s_final, s_prev = lax.scan(step, s0.astype(f32),
                               (jnp.moveaxis(decay, 1, 0), jnp.moveaxis(d_state, 1, 0)))
    s_prev = jnp.moveaxis(s_prev, 0, 1)
    o_inter = jnp.einsum('bnihk,bnhkv->bnihv', qg, s_prev)
    o = (o_intra + o_inter).reshape(B, T, H, DV)
    return o, s_final

def _mixer(x, conv_buf, gla_s, w_in, w_alpha2, b_alpha, conv_w, gla_norm_g, w_out):
    B, T, _ = x.shape
    proj = x @ w_in
    cb, cc, ch, q, k, v, g, a_lr = jnp.split(proj, IN_SPLITS, axis=-1)
    conv_out, new_buf = _short_conv(cc * ch, conv_buf, conv_w)
    y_conv = cb * conv_out
    log_a = jax.nn.log_sigmoid((a_lr @ w_alpha2 + b_alpha).astype(jnp.float32)) / GATE_TEMP
    qh = q.reshape(B, T, GLA_HEADS, GLA_HEAD_K) * (GLA_HEAD_K ** -0.5)
    kh = k.reshape(B, T, GLA_HEADS, GLA_HEAD_K)
    vh = v.reshape(B, T, GLA_HEADS, GLA_HEAD_V)
    ah = log_a.reshape(B, T, GLA_HEADS, GLA_HEAD_K)
    o, new_s = _gla_chunked(qh, kh, vh, ah, gla_s)
    o = o * lax.rsqrt(jnp.mean(jnp.square(o), axis=-1, keepdims=True) + LN_EPS) * gla_norm_g.astype(jnp.float32)
    y_gla = o.reshape(B, T, GLA_DV).astype(x.dtype) * jax.nn.silu(g)
    out = jnp.concatenate([y_conv, y_gla], axis=-1) @ w_out
    return out, new_buf, new_s

def _swiglu(x, w_gate, w_up, w_down):
    return (jax.nn.silu(x @ w_gate) * (x @ w_up)) @ w_down

def _moe(x, router, w_gate, w_up, w_down):
    B, T, D = x.shape
    xf = x.reshape(B * T, D)
    logits = (xf @ router).astype(jnp.float32)
    top_v, top_i = lax.top_k(logits, TOP_K)
    gates = jax.nn.softmax(top_v, axis=-1)
    combine = jnp.sum(jax.nn.one_hot(top_i, N_EXPERTS, dtype=jnp.float32) * gates[..., None], axis=1)
    combine = combine.astype(x.dtype)
    y = jnp.zeros_like(xf)
    for e in range(N_EXPERTS):
        y = y + combine[:, e:e + 1] * _swiglu(xf, w_gate[e], w_up[e], w_down[e])
    return y.reshape(B, T, D)

def _trunk(x, conv_bufs, gla_states, ln_mix_g, ln_mix_b, w_in, w_alpha2, b_alpha, conv_w, gla_norm_g,
           w_out, ln_ffn_g, ln_ffn_b, ffn_w_gate, ffn_w_up, ffn_w_down, moe_router, moe_w_gate,
           moe_w_up, moe_w_down):
    new_states = []
    new_bufs = []
    for l in range(DEPTH):
        m, nb, ns = _mixer(x, conv_bufs[l], gla_states[l], w_in[l], w_alpha2[l], b_alpha[l], conv_w[l],
                           gla_norm_g[l], w_out[l])
        x = _layer_norm(ALPHA * x + m, ln_mix_g[l], ln_mix_b[l])
        if l % 2 == 0:
            f = _swiglu(x, ffn_w_gate[l // 2], ffn_w_up[l // 2], ffn_w_down[l // 2])
        else:
            f = _moe(x, moe_router[l // 2], moe_w_gate[l // 2], moe_w_up[l // 2], moe_w_down[l // 2])
        x = _layer_norm(ALPHA * x + f, ln_ffn_g[l], ln_ffn_b[l])
        new_states.append(ns)
        new_bufs.append(nb)
    return x, jnp.stack(new_states), jnp.stack(new_bufs)

def setup_inputs(seed: int = 0) -> dict:
    key = jax.random.key(seed)
    ks = jax.random.split(key, 24)
    f32 = jnp.float32

    def nrm(k, shape, scale):
        return jax.random.normal(k, shape, f32) * scale

    return {
        "x_prompt": nrm(ks[0], (BATCH, SEQ, D_MODEL), 1.0),
        "x_sample": nrm(ks[1], (DEC_BATCH, DEC_SEQ, D_MODEL), 1.0),
        "cache_conv": nrm(ks[2], (DEPTH, DEC_BATCH, CONV_W - 1, CONV_DIM), 1.0),
        "state_gla": nrm(ks[3], (DEPTH, DEC_BATCH, GLA_HEADS, GLA_HEAD_K, GLA_HEAD_V), 0.5),
        "ln_mix_g": 1.0 + nrm(ks[4], (DEPTH, D_MODEL), 0.02),
        "ln_mix_b": nrm(ks[5], (DEPTH, D_MODEL), 0.02),
        "w_in": nrm(ks[6], (DEPTH, D_MODEL, IN_COLS), D_MODEL ** -0.5),
        "w_alpha2": nrm(ks[7], (DEPTH, GATE_RANK, GLA_QK), GATE_RANK ** -0.5),
        "b_alpha": nrm(ks[8], (DEPTH, GLA_QK), 0.1),
        "conv_w": nrm(ks[9], (DEPTH, CONV_W, CONV_DIM), CONV_W ** -0.5),
        "gla_norm_g": 1.0 + nrm(ks[10], (DEPTH, GLA_HEAD_V), 0.02),
        "w_out": nrm(ks[11], (DEPTH, D_MIX, D_MODEL), BETA * D_MIX ** -0.5),
        "ln_ffn_g": 1.0 + nrm(ks[12], (DEPTH, D_MODEL), 0.02),
        "ln_ffn_b": nrm(ks[13], (DEPTH, D_MODEL), 0.02),
        "ffn_w_gate": nrm(ks[14], (N_DENSE, D_MODEL, D_FF), D_MODEL ** -0.5),
        "ffn_w_up": nrm(ks[15], (N_DENSE, D_MODEL, D_FF), D_MODEL ** -0.5),
        "ffn_w_down": nrm(ks[16], (N_DENSE, D_FF, D_MODEL), BETA * D_FF ** -0.5),
        "moe_router": nrm(ks[17], (N_MOE, D_MODEL, N_EXPERTS), D_MODEL ** -0.5),
        "moe_w_gate": nrm(ks[18], (N_MOE, N_EXPERTS, D_MODEL, D_FF), D_MODEL ** -0.5),
        "moe_w_up": nrm(ks[19], (N_MOE, N_EXPERTS, D_MODEL, D_FF), D_MODEL ** -0.5),
        "moe_w_down": nrm(ks[20], (N_MOE, N_EXPERTS, D_FF, D_MODEL), BETA * D_FF ** -0.5),
    }

def reference(x_prompt, x_sample, cache_conv, state_gla, ln_mix_g, ln_mix_b, w_in, w_alpha2, b_alpha,
              conv_w, gla_norm_g, w_out, ln_ffn_g, ln_ffn_b, ffn_w_gate, ffn_w_up, ffn_w_down,
              moe_router, moe_w_gate, moe_w_up, moe_w_down):
    weights = (ln_mix_g, ln_mix_b, w_in, w_alpha2, b_alpha, conv_w, gla_norm_g, w_out, ln_ffn_g,
               ln_ffn_b, ffn_w_gate, ffn_w_up, ffn_w_down, moe_router, moe_w_gate, moe_w_up, moe_w_down)
    n_prompt = x_prompt.shape[0]
    conv0 = jnp.zeros((DEPTH, n_prompt, CONV_W - 1, CONV_DIM), x_prompt.dtype)
    gla0 = jnp.zeros((DEPTH, n_prompt, GLA_HEADS, GLA_HEAD_K, GLA_HEAD_V), jnp.float32)
    y_prompt, state_gla_prompt, cache_conv_prompt = _trunk(x_prompt, conv0, gla0, *weights)
    y_sample, state_gla_sample, cache_conv_sample = _trunk(x_sample, cache_conv, state_gla, *weights)
    return (y_prompt, y_sample, state_gla_prompt, cache_conv_prompt, state_gla_sample, cache_conv_sample)


_drawn_inputs = setup_inputs


def setup_inputs(seed=0):
    import zlib

    import numpy as np

    out = dict(_drawn_inputs(seed))
    spreads = {}
    factors = {'gla_norm_g': 6.596}
    for name, (base, spread) in spreads.items():
        noise = np.random.default_rng([zlib.crc32(name.encode()), seed]).standard_normal(out[name].shape)
        drawn = base * np.exp(spread * noise) if base else spread * noise
        out[name] = jnp.asarray(drawn.astype(out[name].dtype))
    for name, factor in factors.items():
        out[name] = (out[name] * factor).astype(out[name].dtype)
    return out
```

```python
from contextlib import ExitStack

import concourse.bass as bass
from concourse import mybir

F32 = mybir.dt.float32
F32R = mybir.dt.float32r
I32 = mybir.dt.int32
ALU = mybir.AluOpType
ACT = mybir.ActivationFunctionType
AXX = mybir.AxisListType.X

P = 128
UNIT = 2048
RAW = 6
SPLIT = 3
AHEAD = SPLIT - 1
LN_EPS = 1e-5


def hybrid_stream_step(nc, x_prompt, x_sample, cache_conv, state_gla, ln_mix_g, ln_mix_b, w_in, w_alpha2,
                       b_alpha, conv_w, gla_norm_g, w_out, ln_ffn_g, ln_ffn_b, ffn_w_gate, ffn_w_up,
                       ffn_w_down, moe_router, moe_w_gate, moe_w_up, moe_w_down,
                       y_prompt, y_sample, state_prompt, cache_prompt, state_sample, cache_sample):
    DEPTH, D, IN_COLS = w_in.shape
    SEQ, DEC = x_prompt.shape[1], x_sample.shape[1]
    T = SEQ + DEC
    _, _, HEADS, DK, DV = state_gla.shape
    CONV_W, CONV = conv_w.shape[1:]
    RANK = w_alpha2.shape[1]
    F = ffn_w_gate.shape[2]
    E = moe_router.shape[2]
    ALPHA = (2 * DEPTH) ** 0.25
    GATE_TEMP = 16.0
    CHUNK = 64
    KT = D // P
    TT = -(-T // P)
    TOK = [min(P, T - P * t) for t in range(TT)]
    NCH = T // CHUNK
    LAST = SEQ // CHUNK
    PAIRS = HEADS * DK // P
    VT = HEADS * DV // P
    CT = CONV // P
    FC = F // 512
    assert DEPTH == 2 and D == 1024 and T == 320 and DEC == CHUNK and SEQ % CHUNK == 0
    assert DV == P and DK == 64 and HEADS == 4 and CONV == 512 and F % 512 == 0 and CONV_W == 3

    CB, CC, CH = 0, CONV, 2 * CONV
    Q = 3 * CONV
    K = Q + HEADS * DK
    V = K + HEADS * DK
    G = V + HEADS * DV
    AL = G + HEADS * DV
    IN_UNITS = [Q, K, V, V + 256, G, G + 256, CC, CH, CB, CC + 256, CH + 256, CB + 256]
    TQ, TK, TV, TG = 0, 2, 4, 8
    TCC, TCH, TCB = (12, 18), (14, 20), (16, 22)

    U_IN = [0, 58]
    U_OUT = [12, 70]
    U_FFN = 16
    U_MOE = 74
    PER_CHUNK = 6
    PER_ITEM = PER_CHUNK * FC
    assert PER_CHUNK % RAW == 0 and PER_CHUNK % SPLIT == 0
    assert U_IN[1] == U_FFN + PER_CHUNK * FC

    MORE = 4
    SLOTS = E + MORE + 1

    ITEM = []
    for c in range(FC):
        ITEM.append(("gate", c, 0))
        if c:
            ITEM.append(("T", c - 1, 0))
        ITEM.append(("gate", c, 1))
        if 1 <= c <= KT // 2:
            ITEM.append(("S", 2 * (c - 1), 0))
        ITEM.append(("up", c, 0))
        if 1 <= c <= KT // 2:
            ITEM.append(("S", 2 * (c - 1) + 1, 0))
        if c == KT // 2 + 1:
            ITEM.append(("GT", 0, 0))
        ITEM.append(("up", c, 1))
        if c:
            ITEM += [("down", c - 1, 0), ("down", c - 1, 1)]
    ITEM += [("X", g, 0) for g in range(KT // 2)]
    ITEM += [("T", FC - 1, 0), ("down", FC - 1, 0), ("down", FC - 1, 1)]
    UNITS = [s for s in ITEM if s[0] in ("gate", "up", "down")]
    JOBS = [s for s in ITEM if s[0] in ("T", "S", "GT", "X")]
    PER_JOBS = len(JOBS)
    assert len(UNITS) == PER_ITEM and PER_JOBS % 2 == 0

    ctx = ExitStack()
    with ctx:
        def sb(name, shape, dt=F32):
            return ctx.enter_context(nc.sbuf_tensor(name, shape, dt))

        def sem(name):
            return ctx.enter_context(nc.semaphore(name))

        raw = sb("raw", [P, RAW * UNIT])
        whi = sb("whi", [P, SPLIT * UNIT], F32R)
        wlo = sb("wlo", [P, SPLIT * UNIT], F32R)
        x = sb("x", [P, KT, T])
        ident = sb("ident", [P, P])
        mean_d = sb("mean_d", [P, P])
        mean_v = sb("mean_v", [P, P])
        ones = sb("ones", [P, P])
        before = sb("before", [P, P])
        slot_no = sb("slot_no", [P, P])
        lower_e = sb("lower_e", [P, E, E])
        keep = sb("keep", [P, T])
        causal = sb("causal", [P, P], I32)
        cst = sb("cst", [P, 2])
        N_PRM = 4 * DEPTH * KT + DEPTH * PAIRS + DEPTH * CONV_W * CT + DEPTH + DEPTH * (CONV_W - 1) * CT
        prow = sb("prow", [N_PRM, P])
        prm = sb("prm", [P, N_PRM])
        w_lr = sb("w_lr", [P, DEPTH, KT, RANK])
        w_a2 = sb("w_a2", [RANK, DEPTH, HEADS * DK])
        w_rt = sb("w_rt", [P, KT, E])
        u_mem = sb("u_mem", [P, CT * (T + 2 * (CONV_W - 1))])
        u_ext = u_mem[:, :].rearrange("p (t c) -> p t c", t=CT)
        sq = u_mem[:, 0:4 * T].rearrange("p (t c) -> p t c", t=4)
        more_no = sb("more_no", [P, MORE + 1, 2 * E])
        exp_no = sb("exp_no", [P, 2, E])
        rstd = sb("rstd", [P, T])

        o_mix_g, o_mix_b, o_ffn_g, o_ffn_b = (n * DEPTH * KT for n in range(4))
        o_ba = 4 * DEPTH * KT
        o_cw = o_ba + DEPTH * PAIRS
        o_gn = o_cw + DEPTH * CONV_W * CT
        o_cc = o_gn + DEPTH

        early = ExitStack()

        def sbe(name, shape, dt=F32):
            return early.enter_context(nc.sbuf_tensor(name, shape, dt))

        xh = sbe("xh", [P, KT, T], F32R)
        xl = sbe("xl", [P, KT, T], F32R)
        mix = ExitStack()

        def sbm(name, shape, dt=F32):
            return mix.enter_context(nc.sbuf_tensor(name, shape, dt))

        proj = sbm("proj", [P, 24, T])
        x_in = proj[:, :, :].rearrange("p a b -> p (a b)")[:, 0:TT * D].rearrange("p (t d) -> p t d", t=TT)
        lrT = sbm("lrT", [RANK, T])
        ga = sbm("ga", [P, PAIRS, T])
        og = sbm("og", [P, HEADS, T])
        gb = og[:, 0:PAIRS, :]
        gc = og[:, PAIRS:2 * PAIRS, :]
        kg = sbm("kg", [P, PAIRS, T])
        v_tok = sbm("v_tok", [P, TT, HEADS * DV])
        kd_tok = sbm("kd_tok", [P, TT * HEADS * DK])
        kd_t = kd_tok[:, :].rearrange("p (t c) -> p t c", t=TT)
        CVW = T + CONV_W - 1
        conv = kd_tok[:, 0:2 * CVW].rearrange("p (a c) -> p a c", a=2)
        score = sbm("score", [P, TT, HEADS, P])
        given = sbm("given", [P, DEPTH, PAIRS, DV])
        S_NEW = LAST + 1
        state = sbm("state", [P, PAIRS, LAST + 2, DV])
        rows = sbm("rows", [P, 2, CONV_W - 1, CT])
        rowsT = sbm("rowsT", [2 * (CONV_W - 1) * CT, P])
        mix.close()
        dense = ExitStack()

        def sbd(name, shape, dt=F32):
            return dense.enter_context(nc.sbuf_tensor(name, shape, dt))

        silu_g = sbd("silu_g", [P, 2, T])
        hid = sbd("hid", [P, 2, T])
        hh = sbd("hh", [P, 4, T], F32R)
        hl = sbd("hl", [P, 4, T], F32R)
        dense.close()
        early.close()
        late = ExitStack()
        ctx.enter_context(late)

        def sbl(name, shape, dt=F32):
            return late.enter_context(nc.sbuf_tensor(name, shape, dt))

        xt_hi = sbl("xt_hi", [P, TT, D], F32R)
        xt_lo = sbl("xt_lo", [P, TT, D], F32R)
        xg = sbl("xg", [P, KT, 2, P], F32R)
        sg = sbl("sg", [P, 2, 512])
        hm = sbl("hm", [P, 2, 512])
        hT_hi = sbl("hT_hi", [P, 4, P], F32R)
        hT_lo = sbl("hT_lo", [P, 4, P], F32R)
        pick = sbl("pick", [P, TT, P], F32R)
        pickT = sbl("pickT", [P, T], F32R)
        g_col = sbl("g_col", [P, TT])
        g_slot = sbl("g_slot", [P, 2])
        ys = sbl("ys", [P, D])
        ys_hi = sbl("ys_hi", [P, D], F32R)
        ys_lo = sbl("ys_lo", [P, D], F32R)
        lg = sbl("lg", [P, TT, E])
        cmp_gt = sbl("cmp_gt", [P, TT, E, E])
        cmp_eq = sbl("cmp_eq", [P, TT, E, E])
        rank = sbl("rank", [P, TT, E])
        sel1 = sbl("sel1", [P, TT, E])
        sel2 = sbl("sel2", [P, TT, E])
        sel = sbl("sel", [P, TT, E])
        tmp_e = sbl("tmp_e", [P, TT, E])
        top = sbl("top", [P, 4, TT])
        gat = sbl("gat", [P, 2, TT])
        comb = sbl("comb", [P, TT, E])
        qpos = sbl("qpos", [P, TT, E])
        over = sbl("over", [P, 2, E])
        over_n = sbl("over_n", [P, 2 * E])
        over_i = sbl("over_i", [P, 2 * E])
        slot_of = sbl("slot_of", [P, MORE + 1, 2 * E])
        qsh = sbl("qsh", [P, TT, 2 * E])
        csh = sbl("csh", [P, TT, 2 * E])
        wide = sbl("wide", [P, TT * (MORE + 1), 2 * E])
        q_tab = sbl("q_tab", [P, TT, SLOTS])
        g_tab = sbl("g_tab", [P, TT, SLOTS])
        ctl_f = sbl("ctl_f", [P, 16])
        ctl = sbl("ctl", [1, 16], I32)
        y_tok = sbl("y_tok", [P, TT, D])

        ps = [ctx.enter_context(nc.psum_tensor(f"ps{b}", [P, 512], F32)) for b in range(8)]

        raw_landed = [sem(f"raw_landed{r}") for r in range(RAW)]
        hi_ready, lo_ready, unit_used = sem("hi_ready"), sem("lo_ready"), sem("unit_used")
        prm_landed, x_landed, small_landed, state_landed = (sem(n) for n in (
            "prm_landed", "x_landed", "small_landed", "state_landed"))
        const_step, const_ready = sem("const_step"), sem("const_ready")
        prm_turned, prm_ready, x_turned = sem("prm_turned"), sem("prm_ready"), sem("x_turned")
        x_ready, xh_ready, xl_ready = sem("x_ready"), sem("xh_ready"), sem("xl_ready")
        tile_done = sem("tile_done")
        mean_done, centered, squared, var_part, ln_var, rstd_ready, scaled = (sem(n) for n in (
            "mean_done", "centered", "squared", "var_part", "ln_var", "rstd_ready", "scaled"))
        by_layer = lambda name: [sem(f"{name}{l}") for l in range(DEPTH)]
        proj_ready, lr_done, lr_ready, z_done, gate_act, gate_dve = (by_layer(n) for n in (
            "proj_ready", "lr_done", "lr_ready", "z_done", "gate_act", "gate_dve"))
        kd_turned, v_turned, kd_read, v_read, score_done, score_read = (by_layer(n) for n in (
            "kd_turned", "v_turned", "kd_read", "v_read", "score_done", "score_read"))
        ds_done, st_step, o_done, o_read, o_sq, ms_done, ms_act, og_step = (by_layer(n) for n in (
            "ds_done", "st_step", "o_done", "o_read", "o_sq", "ms_done", "ms_act", "og_step"))
        silu_done, cv_step, y_conv, rows_ready, rows_turned, rowsT_ready, yh_ready, yl_ready, r_ready = (
            by_layer(n) for n in ("silu_done", "cv_step", "y_conv", "rows_ready", "rows_turned", "rowsT_ready",
                                  "yh_ready", "yl_ready", "r_ready"))
        d_silu, d_hid, d_hh, d_hl, d_added = (sem(n) for n in ("d_silu", "d_hid", "d_hh", "d_hl", "d_added"))
        lg_done, xt_done, xth_ready, xtl_ready, rt_step, rt_exp, sel_ready, pos_done, ctl_ready = (sem(n) for n in (
            "lg_done", "xt_done", "xth_ready", "xtl_ready", "rt_step", "rt_exp", "sel_ready", "pos_done",
            "ctl_ready"))
        x_scaled, zeroed, pick_step, pick_ready = (sem(n) for n in ("x_scaled", "zeroed", "pick_step", "pick_ready"))
        job_done, job_read, m_silu, m_hid, hT_hi_ready = (sem(n) for n in (
            "job_done", "job_read", "m_silu", "m_hid", "hT_hi_ready"))
        ys_part, ys_ready, ys_hi_ready, ys_lo_ready = (sem(n) for n in (
            "ys_part", "ys_ready", "ys_hi_ready", "ys_lo_ready"))
        y_turned, y_ready_a, y_ready_v, stored = (sem(n) for n in ("y_turned", "y_ready_a", "y_ready_v", "stored"))

        def slot(t, n, ring, a):
            return t[:, (n % ring) * UNIT:(n % ring + 1) * UNIT].rearrange("p (a c) -> p a c", a=a)

        def flat(t, n, ring):
            return t[:, (n % ring) * UNIT:(n % ring + 1) * UNIT]

        def upto(n, i, per):
            return n if i is None else i * per + n

        ST_STEPS = 1 + PAIRS * (NCH - 1)
        LAYER_STORES = 2 + 2 * PAIRS
        GD_Q, GD_KD = 7, 8
        TD_IN, TD_OUT = [0, 65], [12, 77]
        TD_FFN, TD_CHUNK = 16, 7
        UNITS_OUT = 4
        RT_DIFF = 20
        SMALL_LOADS = 3
        GATHERS = KT // 2
        Y_ORDER = [4, 5, 6, 7, 0, 1, 2, 3]

        def og_tile(k):
            if k >= CT:
                return og[:, k - CT, :]
            return proj[:, TCB[k // 2] + k % 2, :]

        block = ctx.enter_context(nc.Block())

        @block.sync
        def _(sp):
            def load(n, src, a, i=None, per=0):
                if n >= RAW:
                    sp.wait_ge(lo_ready, upto(n - RAW + 1, i, per))
                sp.dma_start(slot(raw, n, RAW, a), src).then_inc(raw_landed[n % RAW], 16)

            def layer_units(l):
                for j, col in enumerate(IN_UNITS):
                    load(U_IN[l] + j, w_in[l, :, col:col + 256].rearrange("(k p) c -> p k c", p=P), KT)
                for j in range(4):
                    load(U_OUT[l] + j, w_out[l, :, 256 * j:256 * j + 256].rearrange("(k p) c -> p k c", p=P), KT)

            layer_units(0)
            with sp.Fori(0, FC) as c:
                for j in range(4):
                    w = (ffn_w_gate, ffn_w_up)[j % 2]
                    col = sp.snap(c * 512 + (j // 2) * 256)
                    load(U_FFN + j, w[0, :, bass.ds(col, 256)].rearrange("(k p) c -> p k c", p=P), KT, c, PER_CHUNK)
                for j in range(2):
                    row = sp.snap(c * 512)
                    load(U_FFN + 4 + j, ffn_w_down[0, bass.ds(row, 512), 512 * j:512 * j + 512].rearrange(
                        "(k p) c -> p k c", p=P), 4, c, PER_CHUNK)
            layer_units(1)

            def item_units(i, e):
                for j, (part, c, half) in enumerate(UNITS):
                    if part == "down":
                        src = moe_w_down[0, bass.ds(e, 1), 512 * c + 256 * half:512 * c + 256 * half + 256, :].rearrange(
                            "e (k p) d -> p (e k) d", p=P)
                        load(U_MOE + j, src, 2, i, PER_ITEM)
                    else:
                        w = moe_w_gate if part == "gate" else moe_w_up
                        src = w[0, bass.ds(e, 1), 512 * half:512 * half + 512, 512 * c:512 * c + 512].rearrange(
                            "e (k p) d -> p (e k) d", p=P)
                        load(U_MOE + j, src, 4, i, PER_ITEM)

            with sp.Fori(0, E) as i:
                item_units(i, i)
            sp.wait_ge(ctl_ready, 1)
            items = sp.value_load(ctl[0:1, MORE + 1:MORE + 2], min_val=E, max_val=E + MORE)
            with sp.If(items > E):
                with sp.Fori(E, items) as i:
                    e = sp.value_load(ctl[0:1, bass.ds(i - E, 1)], min_val=0, max_val=E - 1)
                    item_units(i, e)
            for j in range(AHEAD):
                n = U_MOE + j
                sp.wait_ge(lo_ready, items * PER_ITEM + (n - RAW + 1))
                sp.dma_start(slot(raw, n, RAW, 4), moe_w_gate[0, 0, 0:512, 0:512].rearrange(
                    "(k p) c -> p k c", p=P)).then_inc(raw_landed[n % RAW], 16)

        @block.gpsimd
        def _(pool):
            done = 0

            def const(ins):
                nonlocal done
                done += 1
                ins.then_inc(const_step, 1)
                pool.wait_ge(const_step, done)

            const(pool.memset(ident[:], 0.0))
            const(pool.affine_select(out=ident[:], in_=ident[:], compare_op=ALU.not_equal, fill=1.0, base=0,
                                     pattern=[[-1, P]], channel_multiplier=1))
            const(pool.memset(mean_d[:], 1.0 / D))
            const(pool.memset(mean_v[:], 1.0 / DV))
            const(pool.memset(ones[:], 1.0))
            const(pool.memset(cst[:, 0:1], LN_EPS))
            const(pool.memset(cst[:, 1:2], 1.0))
            const(pool.memset(keep[:], 1.0))
            const(pool.memset(keep[:].rearrange("p (c t) -> p c t", t=CHUNK)[:, :, 0:1], 0.0))
            const(pool.affine_select(out=before[:], in_=ones[:], compare_op=ALU.is_gt, fill=0.0, base=0,
                                     pattern=[[1, P]], channel_multiplier=-1))
            const(pool.memset(lower_e[:], 1.0))
            const(pool.affine_select(out=lower_e[:], in_=lower_e[:], compare_op=ALU.is_gt, fill=0.0, base=0,
                                     pattern=[[1, E], [-1, E]], channel_multiplier=0))
            const(pool.iota(more_no[:], pattern=[[1, MORE + 1], [0, 2 * E]], base=E, channel_multiplier=0,
                            allow_small_or_imprecise_dtypes=True))
            const(pool.iota(exp_no[:], pattern=[[0, 2], [1, E]], base=0, channel_multiplier=0,
                            allow_small_or_imprecise_dtypes=True))
            const(pool.iota(slot_no[:], pattern=[[1, P]], base=1, channel_multiplier=0,
                            allow_small_or_imprecise_dtypes=True))
            const(pool.memset(causal[:], 1))
            const(pool.affine_select(out=causal[:], in_=causal[:], compare_op=ALU.is_ge, fill=0.0, base=0,
                                     pattern=[[1, P]], channel_multiplier=-1))
            const(pool.memset(causal[0:CHUNK, CHUNK:P], 0))
            pool.memset(v_tok[CHUNK:P, TT - 1, :], 0.0).then_inc(const_ready, 1)

            def store(dst, src):
                pool.dma_start(dst, src).then_inc(stored, 16)

            for l in range(DEPTH):
                pool.wait_ge(rowsT_ready[l], 1)
                n = (CONV_W - 1) * CT
                store(cache_prompt[l, 0].rearrange("r (t p) -> (r t) p", p=P), rowsT[0:n, :])
                store(cache_sample[l, 0].rearrange("r (t p) -> (r t) p", p=P), rowsT[n:2 * n, :])
                pool.wait_ge(st_step[l], ST_STEPS)
                for h in range(PAIRS):
                    store(state_prompt[l, 0, 2 * h:2 * h + 2].rearrange("a k v -> (a k) v"), state[:, h, LAST, :])
                    store(state_sample[l, 0, 2 * h:2 * h + 2].rearrange("a k v -> (a k) v"), state[:, h, S_NEW, :])
            for t in range(TT):
                pool.wait_ge(y_ready_a, t + 1)
                pool.wait_ge(y_ready_v, t + 1)
                dst = y_prompt[0, P * t:P * t + P, :] if t < TT - 1 else y_sample[0, :, :]
                store(dst, y_tok[0:TOK[t], t, :])
            pool.wait_ge(stored, 16 * (LAYER_STORES * DEPTH + TT))


        @block.tensor
        def _(pe):
            def split_product(out, pairs, start, stop):
                for j, (wh, wl, hi, lo) in enumerate(pairs):
                    pe.matmul(out, wh, hi, start=start and j == 0, stop=False)
                    pe.matmul(out, wh, lo, start=False, stop=False)
                    mm = pe.matmul(out, wl, hi, start=False, stop=stop and j == len(pairs) - 1)
                return mm

            def by_tile(n, a, half, ks=range(KT), xa=xh, xb=xl):
                cols = slice(P * half, P * half + P)
                return [(slot(whi, n, SPLIT, a)[:, k, cols], slot(wlo, n, SPLIT, a)[:, k, cols],
                         xa[:, k, :], xb[:, k, :]) for k in ks]

            pe.wait_ge(const_ready, 1)
            pe.wait_ge(prm_landed, 16 * 8)
            pe.transpose(ps[0][:, 0:N_PRM], prow[:, :], ident[0:N_PRM, 0:N_PRM]).then_inc(prm_turned, 1)
            pe.wait_ge(x_landed, 16 * TT)
            for k in range(KT):
                if k >= 4:
                    pe.wait_ge(x_ready, k - 3)
                for t in range(TT):
                    mm = pe.transpose(ps[4 + k % 4][:, P * t:P * t + TOK[t]],
                                      x_in[0:TOK[t], t, P * k:P * k + P], ident[0:TOK[t], 0:TOK[t]])
                mm.then_inc(x_turned, 1)

            def norm(stage, wait_residual):
                for k in range(KT):
                    wait_residual(k)
                    mm = pe.matmul(ps[4][:, 0:T], mean_d[:], x[:, k, :], start=k == 0, stop=k == KT - 1)
                mm.then_inc(mean_done, 1)
                for k in range(KT):
                    pe.wait_ge(squared, KT * stage + k + 1)
                    pe.matmul(ps[5][:, 0:T], mean_d[:], sq[:, k % 4, :], start=k == 0, stop=k == KT - 1
                              ).then_inc(var_part, 1)

            def mixer(l):
                def gates():
                    pe.wait_ge(lr_ready[l], 1)
                    for h in range(PAIRS):
                        pe.matmul(ps[5 + h][:, 0:T], w_a2[:, l, P * h:P * h + P], lrT[:, :],
                                  start=True, stop=True).then_inc(z_done[l], 1)

                def turn_kv():
                    pe.wait_ge(gate_dve[l], GD_KD)
                    for t in range(TT):
                        for h in range(PAIRS):
                            at = (t % 2) * 256 + P * h
                            mm = pe.transpose(ps[4 + t // 2][0:TOK[t], at:at + P],
                                              proj[:, TK + h, P * t:P * t + TOK[t]], ident[:])
                        if t >= TT - 2:
                            mm.then_inc(kd_turned[l], 1)
                    pe.wait_ge(proj_ready[l], TV + VT)
                    for t in range(2):
                        for h in range(VT):
                            mm = pe.transpose(ps[6 + t][:, P * h:P * h + P], proj[:, TV + h, P * t:P * t + P],
                                              ident[:])
                        mm.then_inc(v_turned[l], 1)

                def scores():
                    pe.wait_ge(v_read[l], 1)
                    for h in range(VT):
                        mm = pe.transpose(ps[6][0:DEC, P * h:P * h + P], proj[:, TV + h, 2 * P:T], ident[:])
                    mm.then_inc(v_turned[l], 1)
                    pe.wait_ge(kd_read[l], 2)
                    for par in range(2):
                        r = slice(DK * par, DK * par + DK)
                        for n, (t, h) in enumerate((t, h) for t in range(2) for h in range(par, HEADS, 2)):
                            mm = pe.matmul(ps[4 + par][:, P * n:P * n + P], kg[r, h // 2, P * t:P * t + P],
                                           proj[r, TQ + h // 2, P * t:P * t + P], start=True, stop=True)
                        mm.then_inc(score_done[l], 1)

                def chunk_state(c, bank, at):
                    r = slice(CHUNK * (c % 2), CHUNK * (c % 2) + CHUNK)
                    for h in range(HEADS):
                        o = slice(DK * (h % 2), DK * (h % 2) + DK)
                        col = at + DV * (h // 2)
                        mm = pe.matmul(bank[o, col:col + DV], kd_t[r, c // 2, DK * h:DK * h + DK],
                                       v_tok[r, c // 2, DV * h:DV * h + DV], start=True, stop=True)
                    return mm

                def states():
                    for par in range(2):
                        pe.wait_ge(score_read[l], par + 1)
                        r = slice(DK * par, DK * par + DK)
                        for n, h in enumerate(range(par, HEADS, 2)):
                            mm = pe.matmul(ps[4 + par][0:DEC, CHUNK * n:CHUNK * n + CHUNK], kg[r, h // 2, 2 * P:T],
                                           proj[r, TQ + h // 2, 2 * P:T], start=True, stop=True)
                        mm.then_inc(score_done[l], 1)
                    pe.wait_ge(v_read[l], 3)
                    for par in range(2):
                        for c in range(par, LAST, 2):
                            mm = chunk_state(c, ps[6 + par], (c // 2) * 256)
                        mm.then_inc(ds_done[l], 1)
                    pe.wait_ge(score_read[l], 3)
                    chunk_state(LAST, ps[4], 0).then_inc(ds_done[l], 1)

                def outputs():
                    pe.wait_ge(st_step[l], ST_STEPS)
                    pe.wait_ge(score_read[l], 4)
                    for h in range(HEADS):
                        r = slice(DK * (h % 2), DK * (h % 2) + DK)
                        for c in range(NCH):
                            cols = slice(CHUNK * c, CHUNK * c + CHUNK)
                            inner = slice(CHUNK * (c % 2), CHUNK * (c % 2) + CHUNK)
                            lone = c == 0
                            mm = pe.matmul(ps[4 + h][:, cols], v_tok[:, c // 2, DV * h:DV * h + DV],
                                           score[:, c // 2, h, inner], start=True, stop=lone)
                            if not lone:
                                s = given[r, l, h // 2, :] if c == LAST else state[r, h // 2, c, :]
                                mm = pe.matmul(ps[4 + h][:, cols], s, proj[r, TQ + h // 2, cols],
                                               start=False, stop=True)
                        mm.then_inc(o_done[l], 1)

                def mean_squares():
                    for h in range(HEADS):
                        pe.wait_ge(o_sq[l], h + 1)
                        pe.matmul(ps[4 + h][:, 0:T], mean_v[:], proj[:, h, :], start=True, stop=True
                                  ).then_inc(ms_done[l], 1)

                hooks = {0: gates, 5: turn_kv, 6: scores, 7: states, 8: outputs, 9: mean_squares}
                pe.wait_ge(x_ready, KT * (1 + 2 * l))
                pe.wait_ge(small_landed, 16 * SMALL_LOADS)
                for k in range(KT):
                    mm = pe.matmul(ps[4][0:RANK, 0:T], w_lr[:, l, k, :], x[:, k, :], start=k == 0, stop=k == KT - 1)
                mm.then_inc(lr_done[l], 1)
                pe.wait_ge(xl_ready, KT * (1 + 2 * l))
                for u in range(12):
                    n = U_IN[l] + u
                    pe.wait_ge(lo_ready, n + 1)
                    for half in range(2):
                        if 2 * u + half >= 4:
                            pe.wait_ge(proj_ready[l], 2 * u + half - 3)
                        mm = split_product(ps[(2 * u + half) % 4][:, 0:T], by_tile(n, KT, half), True, True)
                        mm.then_inc(unit_used if half else tile_done, 1)
                    if u in hooks:
                        hooks[u]()
                for u in range(UNITS_OUT):
                    n = U_OUT[l] + u
                    pe.wait_ge(lo_ready, n + 1)
                    for half in range(2):
                        m = 2 * u + half
                        if m >= 4:
                            pe.wait_ge(r_ready[l], m - 3)
                        products = by_tile(n, KT, half, Y_ORDER)
                        for j in range(KT):
                            if m == 0:
                                pe.wait_ge(yl_ready[l], j + 1)
                            mm = split_product(ps[m % 4][:, 0:T], products[j:j + 1], j == 0, j == KT - 1)
                        mm.then_inc(unit_used if half else tile_done, 1)
                pe.wait_ge(rows_ready[l], 1)
                pe.transpose(ps[6][0:2 * (CONV_W - 1) * CT, 0:P], rows[:, :, :, :].rearrange("p a b c -> p (a b c)"),
                             ident[:]).then_inc(rows_turned[l], 1)
                norm(2 * l, lambda k: pe.wait_ge(r_ready[l], k + 1))

            def dense_mixer():
                pe.wait_ge(xl_ready, 2 * KT)
                with pe.Fori(0, FC) as c:
                    for j in range(4):
                        n, q = U_FFN + j, j // 2
                        pe.wait_ge(lo_ready, upto(n + 1, c, PER_CHUNK))
                        for half in range(2):
                            bank = 2 * (j % 2) + half
                            if q == 0:
                                pe.wait_ge(d_added, upto(4 + bank + 1, c, 8))
                            else:
                                pe.wait_ge(d_hid, upto(half + 1, c, 4))
                            mm = split_product(ps[bank][:, 0:T], by_tile(n, KT, half), True, True)
                            mm.then_inc(unit_used if half else tile_done, 1)
                    n = U_FFN + 4
                    pe.wait_ge(lo_ready, upto(n + 1, c, PER_CHUNK))
                    pe.wait_ge(d_added, upto(4, c, 8))
                    for k in range(4):
                        pe.wait_ge(d_hl, upto(k + 1, c, 4))
                        for m in range(4):
                            wh, wl = (slot(w, n, SPLIT, 4)[:, k, P * m:P * m + P] for w in (whi, wlo))
                            mm = split_product(ps[4 + m][:, 0:T], [(wh, wl, hh[:, k, :], hl[:, k, :])], k == 0, k == 3)
                    mm.then_inc(unit_used, 1)
                    n = U_FFN + 5
                    pe.wait_ge(lo_ready, upto(n + 1, c, PER_CHUNK))
                    for m in range(4):
                        pairs = [(slot(whi, n, SPLIT, 4)[:, k, P * m:P * m + P],
                                  slot(wlo, n, SPLIT, 4)[:, k, P * m:P * m + P], hh[:, k, :], hl[:, k, :])
                                 for k in range(4)]
                        split_product(ps[m][:, 0:T], pairs, True, True).then_inc(unit_used if m == 3 else tile_done, 1)
                norm(1, lambda k: pe.wait_ge(d_added, 8 * FC + k + 1))

            def router():
                pe.wait_ge(x_ready, 4 * KT)
                for t in range(TT):
                    for k in range(KT):
                        mm = pe.matmul(ps[0][0:TOK[t], E * t:E * t + E], x[:, k, P * t:P * t + TOK[t]],
                                       w_rt[:, k, :], start=k == 0, stop=k == KT - 1)
                mm.then_inc(lg_done, 1)
                for j in range(2 * TT):
                    t, half = j // 2, j % 2
                    for k in range(4):
                        mm = pe.transpose(ps[2 + j][0:TOK[t], P * k:P * k + P],
                                          x[:, 4 * half + k, P * t:P * t + TOK[t]], ident[:])
                    mm.then_inc(xt_done, 1)
                pe.wait_ge(sel_ready, 1)
                for t in range(TT):
                    for s in range(t + 1):
                        pe.matmul(ps[1][:, E * t:E * t + E], (before if s == t else ones)[:], sel[:, s, :],
                                  start=s == 0, stop=s == t)
                for t in range(TT):
                    mm = pe.matmul(ps[1][:, E * TT:E * TT + E], ones[:], sel[:, t, :], start=t == 0, stop=t == TT - 1)
                mm.then_inc(pos_done, 1)

            def gather(g, bank):
                for kk in range(2):
                    k = 2 * g + kk
                    for n, xt in enumerate((xt_hi, xt_lo)):
                        at = (2 * kk + n) * P
                        for t in range(TT):
                            mm = pe.matmul(bank[:, at:at + P], xt[:, t, P * k:P * k + P], pick[:, t, :],
                                           start=t == 0, stop=t == TT - 1)
                mm.then_inc(job_done, 1)

            def scatter(k, bank):
                pe.matmul(bank[:, 0:T], ys_hi[:, P * k:P * k + P], pickT[:, :], start=True, stop=False)
                pe.matmul(bank[:, 0:T], ys_lo[:, P * k:P * k + P], pickT[:, :], start=False, stop=True
                          ).then_inc(job_done, 1)

            def experts(items):
                pe.wait_ge(xtl_ready, 2 * TT)
                pe.wait_ge(pick_ready, 1)
                for g in range(GATHERS):
                    if g >= 2:
                        pe.wait_ge(job_read, g - 1)
                    gather(g, ps[6 + g % 2])
                with pe.Fori(0, items) as i:
                    unit, job = 0, GATHERS
                    for part, c, half in ITEM:
                        if part in ("gate", "up"):
                            n = U_MOE + unit
                            unit += 1
                            if half == 0 and part == "gate":
                                if c == 0:
                                    pe.wait_ge(job_read, upto(GATHERS, i, PER_JOBS))
                                pe.wait_ge(m_hid, upto(max(0, c - 1), i, FC))
                            bank = ps[2 * (c % 2) + (part == "up")]
                            pe.wait_ge(lo_ready, upto(n + 1, i, PER_ITEM))
                            for j in range(4):
                                k = 4 * half + j
                                wh, wl = slot(whi, n, SPLIT, 4)[:, j, :], slot(wlo, n, SPLIT, 4)[:, j, :]
                                pe.matmul(bank[:], xg[:, k, 0, :], wh, start=k == 0, stop=False)
                                pe.matmul(bank[:], xg[:, k, 0, :], wl, start=False, stop=False)
                                mm = pe.matmul(bank[:], xg[:, k, 1, :], wh, start=False, stop=k == KT - 1)
                            mm.then_inc(unit_used, 1)
                        elif part == "down":
                            n = U_MOE + unit
                            unit += 1
                            if half == 0:
                                pe.wait_ge(job_read, upto(turned[c], i, PER_JOBS))
                                if c == 0:
                                    pe.wait_ge(ys_ready, upto(0, i, 1))
                            pe.wait_ge(lo_ready, upto(n + 1, i, PER_ITEM))
                            for j in range(2):
                                k = 2 * half + j
                                for hT, ws in ((hT_hi, (whi, wlo)), (hT_lo, (whi,))):
                                    for w in ws:
                                        for d in range(2):
                                            mm = pe.matmul(ps[4 + d][:], hT[:, k, :],
                                                           slot(w, n, SPLIT, 2)[:, j, 512 * d:512 * d + 512],
                                                           start=c == 0 and k == 0 and hT is hT_hi and w is whi,
                                                           stop=c == FC - 1 and k == 3 and hT is hT_lo)
                            mm.then_inc(unit_used, 1)
                        else:
                            bank = ps[6 + job % 2]
                            pe.wait_ge(job_read, upto(job - 1, i, PER_JOBS))
                            job += 1
                            if part == "T":
                                turned[c] = job
                                pe.wait_ge(m_hid, upto(c + 1, i, FC))
                                for f in range(4):
                                    mm = pe.transpose(bank[:, P * f:P * f + P], hm[:, c % 2, P * f:P * f + P], ident[:])
                                mm.then_inc(job_done, 1)
                            elif part == "S":
                                if c == 0:
                                    pe.wait_ge(ys_lo_ready, upto(1, i, 1))
                                scatter(c, bank)
                            elif part == "GT":
                                for t in range(TT):
                                    pe.transpose(bank[:, P * t:P * t + TOK[t]], pick[0:TOK[t], t, :].bitcast(F32),
                                                 ident[0:TOK[t], 0:TOK[t]])
                                for t in range(TT):
                                    mm = pe.matmul(bank[:, T:T + 1], pick[:, t, :].bitcast(F32), g_col[:, t:t + 1],
                                                   start=t == 0, stop=t == TT - 1)
                                mm.then_inc(job_done, 1)
                            else:
                                if c == 0:
                                    pe.wait_ge(pick_ready, upto(2, i, 1))
                                gather(c, bank)
                pe.wait_ge(ys_lo_ready, items + 1)
                for k in range(KT):
                    pe.wait_ge(job_read, items * PER_JOBS + (GATHERS + k - 1))
                    scatter(k, ps[6 + k % 2])
                norm(3, lambda k: pe.wait_ge(job_read, items * PER_JOBS + (GATHERS + k + 1)))

            turned = {}
            mixer(0)
            dense_mixer()
            mixer(1)
            router()
            pe.wait_ge(ctl_ready, 1)
            items = pe.value_load(ctl[0:1, MORE + 1:MORE + 2], min_val=E, max_val=E + MORE)
            experts(items)
            for half in range(2):
                pe.wait_ge(x_ready, 4 * KT + 4 * half + 4)
                for t in range(TT):
                    for k in range(4):
                        mm = pe.transpose(ps[half + 2 * (t % 2) if t < 2 else 6 + half][0:TOK[t], P * k:P * k + P],
                                          x[:, 4 * half + k, P * t:P * t + TOK[t]], ident[:])
                    mm.then_inc(y_turned, 1)

        @block.scalar
        def _(act):
            def round_unit(n, i=None, per=0):
                act.wait_ge(raw_landed[n % RAW], upto(16 * (n // RAW + 1), i, 16 * (per // RAW)))
                if n >= SPLIT:
                    act.wait_ge(unit_used, upto(n - SPLIT + 1, i, per))
                act.activation(flat(whi, n, SPLIT), flat(raw, n, RAW), ACT.Copy).then_inc(hi_ready, 1)

            def per_column(v, n):
                return prm[:, v + n:v + n + 1]

            row = 0
            for v, rows_of in ((ln_mix_g, "l (k p) -> (l k) p"), (ln_mix_b, "l (k p) -> (l k) p"),
                               (ln_ffn_g, "l (k p) -> (l k) p"), (ln_ffn_b, "l (k p) -> (l k) p"),
                               (b_alpha, "l (k p) -> (l k) p"), (conv_w, "l i (k p) -> (l i k) p"),
                               (gla_norm_g, "l p -> l p"), (cache_conv, "l b r (k p) -> (l b r k) p")):
                src = v if v is gla_norm_g else v.rearrange(rows_of, p=P)
                act.dma_start(prow[row:row + src.shape[0], :], src).then_inc(prm_landed, 16)
                row += src.shape[0]
            for t in range(TT):
                src = x_prompt[0, P * t:P * t + P, :] if t < TT - 1 else x_sample[0]
                act.dma_start(x_in[0:TOK[t], t, :], src).then_inc(x_landed, 16)
            act.dma_start(w_lr[:], w_in[:, :, AL:AL + RANK].rearrange("l (k p) r -> p l k r", p=P)
                          ).then_inc(small_landed, 16)
            act.dma_start(w_a2[:], w_alpha2.rearrange("l r c -> r l c")).then_inc(small_landed, 16)
            act.dma_start(w_rt[:], moe_router[0].rearrange("(k p) e -> p k e", p=P)).then_inc(small_landed, 16)
            for l in range(DEPTH):
                for h in range(PAIRS):
                    act.dma_start(given[:, l, h, :], state_gla[l, 0, 2 * h:2 * h + 2].rearrange(
                        "a k v -> (a k) v")).then_inc(state_landed, 16)

            for n in range(AHEAD):
                round_unit(n)
            act.wait_ge(prm_turned, 1)
            act.activation(prm[:], ps[0][:, 0:N_PRM], ACT.Copy).then_inc(prm_ready, 1)
            for k in range(KT):
                act.wait_ge(x_turned, k + 1)
                act.activation(x[:, k, :], ps[4 + k % 4][:, 0:T], ACT.Copy).then_inc(x_ready, 1)
                act.wait_ge(x_ready, k + 1)
                act.activation(xh[:, k, :], x[:, k, :], ACT.Copy).then_inc(xh_ready, 1)
            act.wait_ge(prm_ready, 1)

            def norm(stage, o_b, split):
                for k in range(KT):
                    act.wait_ge(centered, KT * stage + k + 1)
                    if KT * stage + k >= 4:
                        act.wait_ge(var_part, KT * stage + k - 3)
                    act.activation(sq[:, k % 4, :], x[:, k, :], ACT.Square).then_inc(squared, 1)
                act.wait_ge(var_part, KT * stage + KT)
                act.activation(rstd[:], ps[5][:, 0:T], ACT.Ln, bias=cst[:, 0:1]).then_inc(ln_var, 1)
                act.wait_ge(ln_var, stage + 1)
                act.activation(rstd[:], rstd[:], ACT.Exp, scale=-0.5).then_inc(rstd_ready, 1)
                for k in range(KT):
                    act.wait_ge(scaled, KT * stage + k + 1)
                    act.activation(x[:, k, :], x[:, k, :], ACT.Identity, bias=per_column(o_b, KT * (stage // 2) + k)
                                   ).then_inc(x_ready, 1)
                    if split:
                        act.wait_ge(x_ready, KT * (stage + 1) + k + 1)
                        act.activation(xh[:, k, :], x[:, k, :], ACT.Copy).then_inc(xh_ready, 1)

            def mixer(l):
                def z():
                    for h in range(PAIRS):
                        act.wait_ge(z_done[l], h + 1)
                        act.activation(ga[:, h, :], ps[5 + h][:, 0:T], ACT.Identity,
                                       bias=per_column(o_ba, PAIRS * l + h)).then_inc(gate_act[l], 1)

                def softplus():
                    act.wait_ge(gate_dve[l], 1)
                    act.activation(gc, gc, ACT.Exp, scale=-1.0).then_inc(gate_act[l], 1)
                    act.wait_ge(gate_act[l], 3)
                    act.activation(gc, gc, ACT.Ln, bias=cst[:, 1:2]).then_inc(gate_act[l], 1)

                def exps():
                    act.wait_ge(gate_dve[l], 4)
                    act.activation(ga[:], gb, ACT.Exp, scale=1.0 / GATE_TEMP).then_inc(gate_act[l], 1)
                    act.activation(gc, gb, ACT.Exp, scale=-1.0 / GATE_TEMP).then_inc(gate_act[l], 1)

                def exp_rest():
                    act.wait_ge(gate_dve[l], 7)
                    act.activation(gc, gc, ACT.Exp, scale=1.0 / GATE_TEMP).then_inc(gate_act[l], 1)

                def read_v():
                    for t in range(2):
                        act.wait_ge(v_turned[l], t + 1)
                        act.activation(v_tok[:, t, :], ps[6 + t][:], ACT.Copy).then_inc(v_read[l], 1)

                def read_v_sample():
                    act.wait_ge(v_turned[l], 3)
                    act.activation(v_tok[0:DEC, TT - 1, :], ps[6][0:DEC, :], ACT.Copy).then_inc(v_read[l], 1)

                def silu():
                    act.wait_ge(proj_ready[l], TG + VT)
                    act.activation(proj[:, TG:TG + VT, :], proj[:, TG:TG + VT, :], ACT.Silu).then_inc(silu_done[l], 1)

                def squares():
                    act.wait_ge(o_done[l], HEADS)
                    for h in range(HEADS):
                        act.wait_ge(o_read[l], h + 1)
                        act.activation(proj[:, h, :], og[:, h, :], ACT.Square).then_inc(o_sq[l], 1)

                def rsqrt():
                    for h in range(HEADS):
                        act.wait_ge(ms_done[l], h + 1)
                        act.activation(proj[:, TV + h, :], ps[4 + h][:, 0:T], ACT.Ln, bias=cst[:, 0:1]
                                       ).then_inc(ms_act[l], 1)
                    for h in range(HEADS):
                        act.wait_ge(ms_act[l], h + 1)
                        act.activation(proj[:, TV + h, :], proj[:, TV + h, :], ACT.Exp, scale=-0.5
                                       ).then_inc(ms_act[l], 1)

                hooks = {0: [z], 1: [softplus], 2: [exps], 3: [exp_rest], 5: [read_v], 6: [read_v_sample],
                         7: [silu], 8: [squares], 9: [rsqrt]}
                act.wait_ge(lr_done[l], 1)
                act.activation(lrT[:], ps[4][0:RANK, 0:T], ACT.Copy).then_inc(lr_ready[l], 1)
                for u in range(12):
                    n = U_IN[l] + u
                    round_unit(n + AHEAD)
                    for half in range(2):
                        if half:
                            act.wait_ge(unit_used, n + 1)
                        else:
                            act.wait_ge(tile_done, TD_IN[l] + u + 1)
                        act.activation(proj[:, 2 * u + half, :], ps[(2 * u + half) % 4][:, 0:T], ACT.Copy
                                       ).then_inc(proj_ready[l], 1)
                    for hook in hooks.get(u, []):
                        hook()
                act.wait_ge(unit_used, U_IN[l] + 12)
                for k in Y_ORDER:
                    if k >= CT:
                        act.wait_ge(og_step[l], 2 * (k - CT) + 2)
                    else:
                        act.wait_ge(y_conv[l], k + 1)
                    act.activation(xh[:, k, :], og_tile(k), ACT.Copy).then_inc(yh_ready[l], 1)
                for u in range(UNITS_OUT):
                    round_unit(U_OUT[l] + u + AHEAD)
                act.wait_ge(rows_turned[l], 1)
                if l:
                    act.wait_ge(stored, 16 * LAYER_STORES * l)
                act.activation(rowsT[:], ps[6][0:2 * (CONV_W - 1) * CT, 0:P], ACT.Copy).then_inc(rowsT_ready[l], 1)
                norm(2 * l, o_mix_b, l == 0)

            def dense_mixer():
                with act.Fori(0, FC) as c:
                    for j in range(PER_CHUNK):
                        round_unit(U_FFN + j + AHEAD, c, PER_CHUNK)
                        q = j // 2
                        if j in (0, 2):
                            act.wait_ge(d_hid, upto(2 * q, c, 4))
                            for half in range(2):
                                if half:
                                    act.wait_ge(unit_used, upto(U_FFN + j + 1, c, PER_CHUNK))
                                else:
                                    act.wait_ge(tile_done, upto(TD_FFN + j + 1, c, TD_CHUNK))
                                act.activation(silu_g[:, half, :], ps[half][:, 0:T], ACT.Silu).then_inc(d_silu, 1)
                        elif j in (1, 3):
                            for half in range(2):
                                act.wait_ge(d_hid, upto(2 * q + half + 1, c, 4))
                                act.activation(hh[:, 2 * q + half, :], hid[:, half, :], ACT.Copy).then_inc(d_hh, 1)
                norm(1, o_ffn_b, True)

            def router():
                for j in range(2 * TT):
                    t, half = j // 2, j % 2
                    act.wait_ge(xt_done, j + 1)
                    act.activation(xt_hi[0:TOK[t], t, 512 * half:512 * half + 512], ps[2 + j][0:TOK[t], :],
                                   ACT.Copy).then_inc(xth_ready, 1)
                act.wait_ge(rt_step, RT_DIFF)
                act.activation(top[:, 3, :], top[:, 2, :], ACT.Exp).then_inc(rt_exp, 1)

            def experts(items):
                with act.Fori(0, items) as i:
                    unit, job = 0, GATHERS
                    for part, c, half in ITEM:
                        if part in ("gate", "up", "down"):
                            n = U_MOE + unit
                            unit += 1
                            round_unit(n + AHEAD, i, PER_ITEM)
                            if part == "gate" and half:
                                act.wait_ge(unit_used, upto(n + 1, i, PER_ITEM))
                                act.wait_ge(m_hid, upto(max(0, c - 1), i, FC))
                                act.activation(sg[:, c % 2, :], ps[2 * (c % 2)][:], ACT.Silu).then_inc(m_silu, 1)
                        else:
                            job += 1
                            if part == "T":
                                act.wait_ge(job_done, upto(job, i, PER_JOBS))
                                act.activation(hT_hi[:, :, :].rearrange("p f s -> p (f s)"), ps[6 + (job - 1) % 2][:],
                                               ACT.Copy).then_inc(hT_hi_ready, 1)
                            elif part == "GT":
                                slots_known = job
                    act.wait_ge(unit_used, upto(U_MOE + PER_ITEM, i, PER_ITEM))
                    act.wait_ge(job_read, upto(slots_known, i, PER_JOBS))
                    act.wait_ge(ys_lo_ready, upto(1, i, 1))
                    for d in range(2):
                        act.activation(ys[:, 512 * d:512 * d + 512], ps[4 + d][:], ACT.Copy, scale=g_slot[:, 0:1]
                                       ).then_inc(ys_part if d == 0 else ys_ready, 1)
                    act.wait_ge(ys_ready, upto(1, i, 1))
                    act.activation(ys_hi[:], ys[:], ACT.Copy).then_inc(ys_hi_ready, 1)
                norm(3, o_ffn_b, False)

            mixer(0)
            dense_mixer()
            mixer(1)
            router()
            act.wait_ge(ctl_ready, 1)
            items = act.value_load(ctl[0:1, MORE + 1:MORE + 2], min_val=E, max_val=E + MORE)
            experts(items)
            for t in range(TT):
                act.wait_ge(y_turned, t + 1)
                act.activation(y_tok[0:TOK[t], t, 0:512], ps[2 * (t % 2) if t < 2 else 6][0:TOK[t], :], ACT.Copy
                               ).then_inc(y_ready_a, 1)

        @block.vector
        def _(dve):
            def rest_unit(n, i=None, per=0):
                dve.wait_ge(hi_ready, upto(n + 1, i, per))
                dve.tensor_tensor(flat(wlo, n, SPLIT), flat(raw, n, RAW), flat(whi, n, SPLIT).bitcast(F32),
                                  ALU.subtract).then_inc(lo_ready, 1)

            def per_column(v, n):
                return prm[:, v + n:v + n + 1]

            dve.memset(score[:], 0.0)
            for n in range(AHEAD):
                rest_unit(n)
            for k in range(KT):
                dve.wait_ge(xh_ready, k + 1)
                dve.tensor_tensor(xl[:, k, :], x[:, k, :], xh[:, k, :].bitcast(F32), ALU.subtract).then_inc(xl_ready, 1)
            dve.wait_ge(prm_ready, 1)

            def norm(stage, o_g, split):
                dve.wait_ge(mean_done, stage + 1)
                for k in range(KT):
                    dve.tensor_tensor(x[:, k, :], x[:, k, :], ps[4][:, 0:T], ALU.subtract).then_inc(centered, 1)
                dve.wait_ge(rstd_ready, stage + 1)
                for k in range(KT):
                    dve.wait_ge(squared, KT * stage + k + 1)
                    dve.scalar_tensor_tensor(out=x[:, k, :], in0=x[:, k, :],
                                             scalar=per_column(o_g, KT * (stage // 2) + k), in1=rstd[:],
                                             op0=ALU.mult, op1=ALU.mult).then_inc(scaled, 1)
                if split:
                    for k in range(KT):
                        dve.wait_ge(xh_ready, KT * (stage + 1) + k + 1)
                        dve.tensor_tensor(xl[:, k, :], x[:, k, :], xh[:, k, :].bitcast(F32), ALU.subtract
                                          ).then_inc(xl_ready, 1)

            def mixer(l):
                def absolute():
                    dve.wait_ge(gate_act[l], PAIRS)
                    dve.scalar_tensor_tensor(out=gc, in0=ga[:], scalar=-1.0, in1=ga[:], op0=ALU.mult, op1=ALU.max
                                             ).then_inc(gate_dve[l], 1)

                def log_gates():
                    dve.wait_ge(gate_act[l], 4)
                    dve.scalar_tensor_tensor(out=ga[:], in0=ga[:], scalar=0.0, in1=gc, op0=ALU.min,
                                             op1=ALU.subtract).then_inc(gate_dve[l], 1)
                    dve.wait_ge(gate_dve[l], 2)
                    for h in range(PAIRS):
                        dve.tensor_tensor_scan(gb[:, h, :], keep[:], ga[:, h, :], 0.0, ALU.mult, ALU.add
                                               ).then_inc(gate_dve[l], 1)

                def gated_qk():
                    dve.wait_ge(gate_act[l], 6)
                    dve.wait_ge(proj_ready[l], TK + PAIRS)
                    q, k = proj[:, TQ:TQ + PAIRS, :], proj[:, TK:TK + PAIRS, :]
                    dve.scalar_tensor_tensor(out=q, in0=q, scalar=DK ** -0.5, in1=ga[:], op0=ALU.mult, op1=ALU.mult
                                             ).then_inc(gate_dve[l], 1)
                    dve.tensor_tensor(kg[:], k, gc, ALU.mult).then_inc(gate_dve[l], 1)
                    dve.wait_ge(gate_dve[l], 6)
                    b = gb.rearrange("p h (c t) -> p h c t", t=CHUNK)
                    dve.tensor_tensor(gc.rearrange("p h (c t) -> p h c t", t=CHUNK),
                                      b[:, :, :, CHUNK - 1:CHUNK].to_broadcast([P, PAIRS, NCH, CHUNK]), b,
                                      ALU.subtract).then_inc(gate_dve[l], 1)

                def kd():
                    dve.wait_ge(gate_act[l], 7)
                    k = proj[:, TK:TK + PAIRS, :]
                    dve.tensor_tensor(k, k, gc, ALU.mult).then_inc(gate_dve[l], 1)

                def read_kd():
                    dve.wait_ge(kd_turned[l], 1)
                    dve.tensor_copy(kd_tok[:, 0:512], ps[4][:]).then_inc(kd_read[l], 1)
                    dve.wait_ge(kd_turned[l], 2)
                    dve.tensor_copy(kd_tok[0:DEC, 512:768], ps[5][0:DEC, 0:256]).then_inc(kd_read[l], 1)

                def mask_scores():
                    for par in range(2):
                        dve.wait_ge(score_done[l], par + 1)
                        for t in range(2):
                            mm = dve.copy_predicated(
                                score[:, t, par::2, :], causal[:].unsqueeze(1).to_broadcast([P, 2, P]),
                                ps[4 + par][:, 256 * t:256 * t + 256].rearrange("p (h i) -> p h i", h=2))
                        mm.then_inc(score_read[l], 1)

                def state_chain():
                    for par in range(2):
                        dve.wait_ge(score_done[l], 3 + par)
                        dve.copy_predicated(
                            score[0:DEC, TT - 1, par::2, 0:CHUNK],
                            causal[0:DEC, 0:CHUNK].unsqueeze(1).to_broadcast([DEC, 2, CHUNK]),
                            ps[4 + par][0:DEC, 0:2 * CHUNK].rearrange("p (h i) -> p h i", h=2)
                        ).then_inc(score_read[l], 1)
                    if l:
                        dve.wait_ge(stored, 16 * LAYER_STORES * l)
                    dve.wait_ge(ds_done[l], 2)
                    dve.tensor_copy(state[:, :, 1, :], ps[6][:, 0:256].rearrange("p (h v) -> p h v", h=PAIRS)
                                    ).then_inc(st_step[l], 1)
                    done = 1
                    for c in range(1, LAST):
                        dve.wait_ge(st_step[l], done)
                        for h in range(PAIRS):
                            at = (c // 2) * 256 + DV * h
                            last = CHUNK * c + CHUNK - 1
                            dve.scalar_tensor_tensor(
                                out=state[:, h, c + 1, :], in0=state[:, h, c, :], scalar=ga[:, h, last:last + 1],
                                in1=ps[6 + c % 2][:, at:at + DV], op0=ALU.mult, op1=ALU.add).then_inc(st_step[l], 1)
                            done += 1
                    dve.wait_ge(ds_done[l], 3)
                    dve.wait_ge(state_landed, 16 * DEPTH * PAIRS)
                    for h in range(PAIRS):
                        dve.scalar_tensor_tensor(
                            out=state[:, h, S_NEW, :], in0=given[:, l, h, :], scalar=ga[:, h, T - 1:T],
                            in1=ps[4][:, DV * h:DV * h + DV], op0=ALU.mult, op1=ALU.add).then_inc(st_step[l], 1)

                def read_o():
                    for h in range(HEADS):
                        dve.wait_ge(o_done[l], h + 1)
                        dve.tensor_copy(og[:, h, :], ps[4 + h][:, 0:T]).then_inc(o_read[l], 1)

                def weigh_o():
                    dve.wait_ge(silu_done[l], 1)
                    for h in range(HEADS):
                        dve.wait_ge(o_sq[l], h + 1)
                        dve.wait_ge(ms_act[l], HEADS + h + 1)
                        dve.scalar_tensor_tensor(out=og[:, h, :], in0=og[:, h, :], scalar=per_column(o_gn, l),
                                                 in1=proj[:, TV + h, :], op0=ALU.mult, op1=ALU.mult
                                                 ).then_inc(og_step[l], 1)
                        dve.wait_ge(og_step[l], 2 * h + 1)
                        dve.tensor_tensor(og[:, h, :], og[:, h, :], proj[:, TG + h, :], ALU.mult
                                          ).then_inc(og_step[l], 1)

                cv = 0

                def conv_step(ins):
                    nonlocal cv
                    cv += 1
                    ins.then_inc(cv_step[l], 1)
                    return cv

                def conv_pads():
                    if l:
                        dve.wait_ge(var_part, 2 * KT)
                    conv_step(dve.memset(u_ext[:, :, 0:CONV_W - 1], 0.0))
                    at = o_cc + l * (CONV_W - 1) * CT
                    conv_step(dve.tensor_copy(
                        u_ext[:, :, SEQ + CONV_W - 1:SEQ + 2 * (CONV_W - 1)],
                        prm[:, at:at + (CONV_W - 1) * CT].rearrange("p (r t) -> p t r", t=CT)))

                def conv_tiles(g):
                    def run():
                        dve.wait_ge(proj_ready[l], TCH[g] + 2)
                        if g == 0:
                            dve.wait_ge(ds_done[l], 3)
                        for j in range(2):
                            t = 2 * g + j
                            a, b = proj[:, TCC[g] + j, :], proj[:, TCH[g] + j, :]
                            conv_step(dve.tensor_tensor(u_ext[:, t, 2:2 + SEQ], a[:, 0:SEQ], b[:, 0:SEQ], ALU.mult))
                            n = conv_step(dve.tensor_tensor(u_ext[:, t, SEQ + 4:T + 4], a[:, SEQ:T], b[:, SEQ:T],
                                                            ALU.mult))
                            w = o_cw + l * CONV_W * CT + t
                            dve.wait_ge(cv_step[l], n)
                            if g:
                                dve.wait_ge(y_conv[l], j + 1)
                            n = conv_step(dve.tensor_scalar(conv[:, j, :], u_ext[:, t, 0:CVW], per_column(w, 0), None,
                                                            ALU.mult))
                            for tap in range(1, CONV_W):
                                dve.wait_ge(cv_step[l], n)
                                n = conv_step(dve.scalar_tensor_tensor(
                                    out=conv[:, j, :], in0=u_ext[:, t, tap:tap + CVW], scalar=per_column(w, CT * tap),
                                    in1=conv[:, j, :], op0=ALU.mult, op1=ALU.add))
                    return run

                def conv_out(g):
                    def run():
                        dve.wait_ge(cv_step[l], cv)
                        dve.wait_ge(proj_ready[l], TCB[g] + 2)
                        for j in range(2):
                            c = proj[:, TCB[g] + j, :]
                            conv_step(dve.tensor_tensor(c[:, 0:SEQ], c[:, 0:SEQ], conv[:, j, 0:SEQ], ALU.mult))
                            dve.tensor_tensor(c[:, SEQ:T], c[:, SEQ:T], conv[:, j, SEQ + 2:CVW], ALU.mult
                                              ).then_inc(y_conv[l], 1)
                    return run

                hooks = {1: [absolute], 2: [log_gates], 3: [gated_qk], 4: [kd, conv_pads], 5: [read_kd],
                         6: [mask_scores], 7: [state_chain], 8: [read_o, conv_tiles(0)], 9: [conv_out(0)],
                         10: [weigh_o], 11: [conv_tiles(1), conv_out(1)]}
                for u in range(12):
                    rest_unit(U_IN[l] + u + AHEAD)
                    for hook in hooks.get(u, []):
                        hook()
                for j, k in enumerate(Y_ORDER):
                    dve.wait_ge(yh_ready[l], j + 1)
                    dve.tensor_tensor(xl[:, k, :], og_tile(k), xh[:, k, :].bitcast(F32), ALU.subtract
                                      ).then_inc(yl_ready[l], 1)
                dve.tensor_copy(rows[:, 0, :, :], u_ext[:, :, SEQ:SEQ + 2].rearrange("p t r -> p r t"))
                dve.tensor_copy(rows[:, 1, :, :], u_ext[:, :, T + 2:T + 4].rearrange("p t r -> p r t")
                                ).then_inc(rows_ready[l], 1)
                for u in range(UNITS_OUT):
                    n = U_OUT[l] + u
                    rest_unit(n + AHEAD)
                    for half in range(2):
                        m = 2 * u + half
                        if half:
                            dve.wait_ge(unit_used, n + 1)
                        else:
                            dve.wait_ge(tile_done, TD_OUT[l] + u + 1)
                        dve.scalar_tensor_tensor(out=x[:, m, :], in0=x[:, m, :], scalar=ALPHA, in1=ps[m % 4][:, 0:T],
                                                 op0=ALU.mult, op1=ALU.add).then_inc(r_ready[l], 1)
                dve.wait_ge(r_ready[l], KT)
                norm(2 * l, o_mix_g, l == 0)

            def dense_mixer():
                for k in range(KT):
                    dve.tensor_scalar(x[:, k, :], x[:, k, :], ALPHA, None, ALU.mult).then_inc(d_added, 1)
                with dve.Fori(0, FC) as c:
                    for j in range(PER_CHUNK):
                        n, q = U_FFN + j, j // 2
                        rest_unit(n + AHEAD, c, PER_CHUNK)
                        if j in (1, 3):
                            dve.wait_ge(d_hl, upto(2 * q, c, 4))
                            for half in range(2):
                                dve.wait_ge(d_silu, upto(2 * q + half + 1, c, 4))
                                if half:
                                    dve.wait_ge(unit_used, upto(n + 1, c, PER_CHUNK))
                                else:
                                    dve.wait_ge(tile_done, upto(TD_FFN + j + 1, c, TD_CHUNK))
                                dve.tensor_tensor(hid[:, half, :], silu_g[:, half, :], ps[2 + half][:, 0:T], ALU.mult
                                                  ).then_inc(d_hid, 1)
                            for half in range(2):
                                dve.wait_ge(d_hh, upto(2 * q + half + 1, c, 4))
                                dve.tensor_tensor(hl[:, 2 * q + half, :], hid[:, half, :],
                                                  hh[:, 2 * q + half, :].bitcast(F32), ALU.subtract).then_inc(d_hl, 1)
                        elif j >= 4:
                            for m in range(4):
                                if j == 4 or m == 3:
                                    dve.wait_ge(unit_used, upto(n + 1, c, PER_CHUNK))
                                else:
                                    dve.wait_ge(tile_done, upto(TD_FFN + 4 + m + 1, c, TD_CHUNK))
                                k = 4 * (j - 4) + m
                                dve.wait_ge(d_added, upto(k + 1, c, 8))
                                dve.tensor_tensor(x[:, k, :], x[:, k, :], ps[m if j == 5 else 4 + m][:, 0:T], ALU.add
                                                  ).then_inc(d_added, 1)
                dve.wait_ge(d_added, 8 * (FC + 1))
                norm(1, o_ffn_g, True)

            def router():
                n = 0

                def step(ins):
                    nonlocal n
                    n += 1
                    ins.then_inc(rt_step, 1)
                    dve.wait_ge(rt_step, n)
                    return n

                dve.wait_ge(x_ready, 4 * KT)
                step(dve.memset(lg[:], 0.0))
                step(dve.memset(xt_hi[TOK[2]:P, 2, :].bitcast(F32), 0.0))
                step(dve.memset(xt_lo[TOK[2]:P, 2, :].bitcast(F32), 0.0))
                dve.wait_ge(lg_done, 1)
                step(dve.tensor_copy(lg[:, 0:2, :], ps[0][:, 0:2 * E].rearrange("p (t e) -> p t e", e=E)))
                step(dve.tensor_copy(lg[0:TOK[2], 2, :], ps[0][0:TOK[2], 2 * E:3 * E]))
                full = [P, TT, E, E]
                mine = lg[:].unsqueeze(3).to_broadcast(full)
                other = lg[:].unsqueeze(2).to_broadcast(full)
                step(dve.tensor_tensor(cmp_gt[:], other, mine, ALU.is_gt))
                step(dve.tensor_tensor(cmp_eq[:], other, mine, ALU.is_equal))
                step(dve.tensor_tensor(cmp_eq[:].rearrange("p t e f -> p t (e f)"),
                                       cmp_eq[:].rearrange("p t e f -> p t (e f)"),
                                       lower_e[:].rearrange("p e f -> p (e f)").unsqueeze(1).to_broadcast([P, TT, E * E]),
                                       ALU.mult))
                step(dve.tensor_tensor(cmp_gt[:], cmp_gt[:], cmp_eq[:], ALU.add))
                step(dve.tensor_reduce(rank[:], cmp_gt[:], AXX, ALU.add))
                step(dve.tensor_scalar(sel1[:], rank[:], 0.0, None, ALU.is_equal))
                step(dve.tensor_scalar(sel2[:], rank[:], 1.0, None, ALU.is_equal))
                step(dve.memset(sel1[TOK[2]:P, 2, :], 0.0))
                step(dve.memset(sel2[TOK[2]:P, 2, :], 0.0))
                step(dve.tensor_tensor(sel[:], sel1[:], sel2[:], ALU.add))
                dve.memset(g_col[:], 0.0).then_inc(sel_ready, 1)
                for m, s in enumerate((sel1, sel2)):
                    step(dve.tensor_tensor(tmp_e[:], s[:], lg[:], ALU.mult))
                    step(dve.tensor_reduce(top[:, m, :], tmp_e[:], AXX, ALU.add))
                assert n + 1 == RT_DIFF
                step(dve.tensor_tensor(top[:, 2, :], top[:, 1, :], top[:, 0, :], ALU.subtract))
                dve.wait_ge(rt_exp, 1)
                step(dve.tensor_scalar(gat[:, 1, :], top[:, 3, :], 1.0, None, ALU.add))
                step(dve.reciprocal(gat[:, 0, :], gat[:, 1, :]))
                step(dve.tensor_tensor(gat[:, 1, :], top[:, 3, :], gat[:, 0, :], ALU.mult))
                step(dve.tensor_tensor(comb[:], sel1[:], gat[:, 0, :].unsqueeze(2).to_broadcast([P, TT, E]), ALU.mult))
                step(dve.tensor_tensor(tmp_e[:], sel2[:], gat[:, 1, :].unsqueeze(2).to_broadcast([P, TT, E]), ALU.mult))
                step(dve.tensor_tensor(comb[:], comb[:], tmp_e[:], ALU.add))
                dve.wait_ge(pos_done, 1)
                step(dve.scalar_tensor_tensor(out=qpos[:], in0=ps[1][:, 0:TT * E].rearrange("p (t e) -> p t e", e=E),
                                              scalar=1.0, in1=sel[:], op0=ALU.add, op1=ALU.mult))
                for j in range(2):
                    step(dve.tensor_scalar(over[:, j, :], ps[1][:, TT * E:TT * E + E], float(P * (j + 1)), None,
                                           ALU.is_gt))
                flat_over = over[:].rearrange("p j e -> p (j e)")
                step(dve.tensor_tensor_scan(over_n[:], ones[:, 0:2 * E], flat_over, 0.0, ALU.mult, ALU.add))
                step(dve.tensor_scalar(over_i[:], over_n[:], float(E - 1), None, ALU.add))
                shape = [P, MORE + 1, 2 * E]
                step(dve.tensor_tensor(slot_of[:], more_no[:], over_i[:].unsqueeze(1).to_broadcast(shape),
                                       ALU.is_equal))
                step(dve.tensor_tensor(slot_of[:], slot_of[:], flat_over.unsqueeze(1).to_broadcast(shape), ALU.mult))
                for j in range(2):
                    step(dve.tensor_scalar(qsh[:, :, E * j:E * j + E], qpos[:], float(-P * (j + 1)), None, ALU.add))
                    step(dve.tensor_copy(csh[:, :, E * j:E * j + E], comb[:]))
                wide4 = wide[:].rearrange("p (t s) n -> p t s n", t=TT)
                for tab, of, plain in ((q_tab, qsh, qpos), (g_tab, csh, comb)):
                    for t in range(TT):
                        step(dve.tensor_tensor(wide4[:, t], slot_of[:], of[:, t, :].unsqueeze(1).to_broadcast(shape),
                                               ALU.mult))
                    step(dve.tensor_reduce(tab[:, :, E:SLOTS], wide4, AXX, ALU.add))
                    step(dve.tensor_copy(tab[:, :, 0:E], plain[:]))
                step(dve.tensor_tensor(wide4[:, 0], slot_of[:],
                                       exp_no[:].rearrange("p j e -> p (j e)").unsqueeze(1).to_broadcast(shape),
                                       ALU.mult))
                step(dve.tensor_reduce(ctl_f[:, 0:MORE + 1], wide4[:, 0], AXX, ALU.add))
                step(dve.tensor_scalar(ctl_f[:, MORE + 1:MORE + 2], over_n[:, 2 * E - 1:2 * E], float(E), None, ALU.add))
                dve.tensor_copy(ctl[0:1, 0:MORE + 2], ctl_f[0:1, 0:MORE + 2]).then_inc(ctl_ready, 1)
                make_pick(0)
                for j in range(2 * TT):
                    t, half = j // 2, j % 2
                    dve.wait_ge(xth_ready, j + 1)
                    cols = slice(512 * half, 512 * half + 512)
                    dve.tensor_tensor(xt_lo[0:TOK[t], t, cols], ps[2 + j][0:TOK[t], :],
                                      xt_hi[0:TOK[t], t, cols].bitcast(F32), ALU.subtract).then_inc(xtl_ready, 1)
                dve.tensor_scalar(x[:].rearrange("p k t -> p (k t)"), x[:].rearrange("p k t -> p (k t)"), ALPHA, None,
                                  ALU.mult).then_inc(x_scaled, 1)
                dve.memset(pickT[:].bitcast(F32), 0.0)
                dve.memset(ys_hi[:].bitcast(F32), 0.0)
                dve.memset(ys_lo[:].bitcast(F32), 0.0).then_inc(ys_lo_ready, 1)

            def make_pick(i):
                at = slice(i, i + 1) if isinstance(i, int) else bass.ds(i, 1)
                for t in range(TT):
                    dve.tensor_scalar(pick[:, t, :], slot_no[:], q_tab[:, t, at], None, ALU.is_equal)
                dve.tensor_copy(g_col[:].unsqueeze(2), g_tab[:, :, at]).then_inc(pick_ready, 1)

            def experts(items):
                for g in range(GATHERS):
                    dve.wait_ge(job_done, g + 1)
                    dve.tensor_copy(xg[:, 2 * g:2 * g + 2, :, :].rearrange("p k n s -> p (k n s)"), ps[6 + g % 2][:]
                                    ).then_inc(job_read, 1)
                with dve.Fori(0, items) as i:
                    unit, job, chunk = 0, GATHERS, 0
                    for part, c, half in ITEM:
                        if part in ("gate", "up", "down"):
                            n = U_MOE + unit
                            unit += 1
                            rest_unit(n + AHEAD, i, PER_ITEM)
                            if part == "up" and half:
                                dve.wait_ge(unit_used, upto(n + 1, i, PER_ITEM))
                                dve.wait_ge(m_silu, upto(c + 1, i, FC))
                                dve.tensor_tensor(hm[:, c % 2, :], sg[:, c % 2, :], ps[2 * (c % 2) + 1][:], ALU.mult
                                                  ).then_inc(m_hid, 1)
                            continue
                        bank = ps[6 + job % 2]
                        dve.wait_ge(job_done, upto(job + 1, i, PER_JOBS))
                        if part == "T":
                            chunk += 1
                            dve.wait_ge(hT_hi_ready, upto(chunk, i, FC))
                            dve.tensor_tensor(hT_lo[:, :, :].rearrange("p f s -> p (f s)"), bank[:],
                                              hT_hi[:, :, :].rearrange("p f s -> p (f s)").bitcast(F32), ALU.subtract
                                              ).then_inc(job_read, 1)
                        elif part == "S":
                            if c == 0:
                                dve.wait_ge(x_scaled, 1)
                            dve.wait_ge(job_read, upto(job, i, PER_JOBS))
                            dve.tensor_tensor(x[:, c, :], x[:, c, :], bank[:, 0:T], ALU.add).then_inc(job_read, 1)
                        elif part == "GT":
                            dve.wait_ge(ys_ready, upto(0, i, 1))
                            dve.tensor_copy(pickT[:], bank[:, 0:T])
                            dve.tensor_copy(g_slot[:, 0:1], bank[:, T:T + 1]).then_inc(job_read, 1)
                            make_pick(dve.snap(i + 1))
                        else:
                            dve.tensor_copy(xg[:, 2 * c:2 * c + 2, :, :].rearrange("p k n s -> p (k n s)"), bank[:]
                                            ).then_inc(job_read, 1)
                        job += 1
                    dve.wait_ge(ys_hi_ready, upto(1, i, 1))
                    dve.tensor_tensor(ys_lo[:], ys[:], ys_hi[:].bitcast(F32), ALU.subtract).then_inc(ys_lo_ready, 1)
                for k in range(KT):
                    dve.wait_ge(job_done, items * PER_JOBS + (GATHERS + k + 1))
                    dve.wait_ge(job_read, items * PER_JOBS + (GATHERS + k))
                    dve.tensor_tensor(x[:, k, :], x[:, k, :], ps[6 + k % 2][:, 0:T], ALU.add).then_inc(job_read, 1)
                dve.wait_ge(job_read, items * PER_JOBS + (GATHERS + KT))
                norm(3, o_ffn_g, False)

            mixer(0)
            dense_mixer()
            mixer(1)
            router()
            dve.wait_ge(ctl_ready, 1)
            items = dve.value_load(ctl[0:1, MORE + 1:MORE + 2], min_val=E, max_val=E + MORE)
            experts(items)
            for t in range(TT):
                dve.wait_ge(y_turned, TT + t + 1)
                dve.tensor_copy(y_tok[0:TOK[t], t, 512:1024], ps[1 + 2 * (t % 2) if t < 2 else 7][0:TOK[t], :]
                                ).then_inc(y_ready_v, 1)


_INS = ["x_prompt", "x_sample", "cache_conv", "state_gla", "ln_mix_g", "ln_mix_b", "w_in", "w_alpha2", "b_alpha",
        "conv_w", "gla_norm_g", "w_out", "ln_ffn_g", "ln_ffn_b", "ffn_w_gate", "ffn_w_up", "ffn_w_down",
        "moe_router", "moe_w_gate", "moe_w_up", "moe_w_down"]


def kernel(**inputs):
    import numpy as np
    import concourse.bacc as bacc
    from concourse.bass_utils import run_bass_kernel_spmd

    nc = bacc.Bacc("TRN2", target_bir_lowering=False, num_devices=1)
    arrays, args = {}, []
    for name in _INS:
        a = np.ascontiguousarray(inputs[name])
        arrays[f"in_{name}"] = a
        args.append(nc.dram_tensor(f"in_{name}", a.shape, mybir.dt.from_np(a.dtype), kind="ExternalInput").ap())
    depth, _, heads, dk, dv = inputs["state_gla"].shape
    _, _, rows, conv = inputs["cache_conv"].shape
    shapes = [inputs["x_prompt"].shape, inputs["x_sample"].shape,
              (depth, inputs["x_prompt"].shape[0], heads, dk, dv), (depth, inputs["x_prompt"].shape[0], rows, conv),
              inputs["state_gla"].shape, inputs["cache_conv"].shape]
    for i, shape in enumerate(shapes):
        args.append(nc.dram_tensor(f"out_{i}", shape, F32, kind="ExternalOutput").ap())
    hybrid_stream_step(nc, *args)
    r = run_bass_kernel_spmd(nc, [arrays], core_ids=[0])
    return tuple(r.results[0][f"out_{i}"] for i in range(len(shapes)))
```

```python
from contextlib import ExitStack

import concourse.bass as bass
from concourse import mybir

F32 = mybir.dt.float32
F32R = mybir.dt.float32r
I32 = mybir.dt.int32
ALU = mybir.AluOpType
ACT = mybir.ActivationFunctionType
AXX = mybir.AxisListType.X

P = 128
UNIT = 2048
RAW = 6
SPLIT = 3
AHEAD = SPLIT - 1
LN_EPS = 1e-5


def hybrid_stream_step(nc, x_prompt, x_sample, cache_conv, state_gla, ln_mix_g, ln_mix_b, w_in, w_alpha2,
                       b_alpha, conv_w, gla_norm_g, w_out, ln_ffn_g, ln_ffn_b, ffn_w_gate, ffn_w_up,
                       ffn_w_down, moe_router, moe_w_gate, moe_w_up, moe_w_down,
                       y_prompt, y_sample, state_prompt, cache_prompt, state_sample, cache_sample):
    DEPTH, D, IN_COLS = w_in.shape
    SEQ, DEC = x_prompt.shape[1], x_sample.shape[1]
    T = SEQ + DEC
    _, _, HEADS, DK, DV = state_gla.shape
    CONV_W, CONV = conv_w.shape[1:]
    RANK = w_alpha2.shape[1]
    F = ffn_w_gate.shape[2]
    E = moe_router.shape[2]
    ALPHA = (2 * DEPTH) ** 0.25
    GATE_TEMP = 16.0
    CHUNK = 64
    KT = D // P
    TT = -(-T // P)
    TOK = [min(P, T - P * t) for t in range(TT)]
    NCH = T // CHUNK
    LAST = SEQ // CHUNK
    PAIRS = HEADS * DK // P
    VT = HEADS * DV // P
    CT = CONV // P
    FC = F // 512
    assert DEPTH == 2 and D == 1024 and T == 320 and DEC == CHUNK and SEQ % CHUNK == 0
    assert DV == P and DK == 64 and HEADS == 4 and CONV == 512 and F % 512 == 0 and CONV_W == 3

    CB, CC, CH = 0, CONV, 2 * CONV
    Q = 3 * CONV
    K = Q + HEADS * DK
    V = K + HEADS * DK
    G = V + HEADS * DV
    AL = G + HEADS * DV
    IN_UNITS = [Q, K, V, V + 256, G, G + 256, CC, CH, CC + 256, CH + 256, CB, CB + 256]
    TQ, TK, TV, TG = 0, 2, 4, 8
    TCC, TCH, TCB = (12, 16), (14, 18), (20, 22)

    assert (TQ, TV, TG, TCC[0], TCH[0]) == (0, CT, 2 * CT, 3 * CT, 3 * CT + 2)

    U_IN = [0, 58]
    U_OUT = [12, 70]
    U_FFN = 16
    U_MOE = 74
    PER_CHUNK = 6
    PER_ITEM = PER_CHUNK * FC
    assert PER_CHUNK % RAW == 0 and PER_CHUNK % SPLIT == 0
    assert U_IN[1] == U_FFN + PER_CHUNK * FC

    MORE = 4
    SLOTS = E + MORE + 1

    ITEM = []
    for c in range(FC):
        ITEM.append(("gate", c, 0))
        if c:
            ITEM.append(("T", c - 1, 0))
        ITEM.append(("gate", c, 1))
        if 1 <= c <= KT // 2:
            ITEM.append(("S", 2 * (c - 1), 0))
        ITEM.append(("up", c, 0))
        if 1 <= c <= KT // 2:
            ITEM.append(("S", 2 * (c - 1) + 1, 0))
        if c == KT // 2 + 1:
            ITEM.append(("GT", 0, 0))
        ITEM.append(("up", c, 1))
        if c:
            ITEM += [("down", c - 1, 0), ("down", c - 1, 1)]
    ITEM += [("X", 0, 0), ("X", 1, 0), ("T", FC - 1, 0), ("X", 2, 0), ("X", 3, 0)]
    ITEM += [("down", FC - 1, 0), ("down", FC - 1, 1)]
    UNITS = [s for s in ITEM if s[0] in ("gate", "up", "down")]
    JOBS = [s for s in ITEM if s[0] in ("T", "S", "GT", "X")]
    PER_JOBS = len(JOBS)
    assert len(UNITS) == PER_ITEM and PER_JOBS % 2 == 0

    ctx = ExitStack()
    with ctx:
        def sb(name, shape, dt=F32):
            return ctx.enter_context(nc.sbuf_tensor(name, shape, dt))

        def sem(name):
            return ctx.enter_context(nc.semaphore(name))

        raw = sb("raw", [P, RAW * UNIT])
        whi = sb("whi", [P, SPLIT * UNIT], F32R)
        wlo = sb("wlo", [P, SPLIT * UNIT], F32R)
        x = sb("x", [P, KT, T])
        ident = sb("ident", [P, P])
        mean_d = sb("mean_d", [P, P])
        mean_v = sb("mean_v", [P, P])
        ones = sb("ones", [P, P])
        before = sb("before", [P, P])
        slot_no = sb("slot_no", [P, P])
        lower_e = sb("lower_e", [P, E, E])
        keep = sb("keep", [P, T])
        causal = sb("causal", [P, P], I32)
        cst = sb("cst", [P, 2])
        N_PRM = 4 * DEPTH * KT + DEPTH * PAIRS + DEPTH * CONV_W * CT + DEPTH + DEPTH * (CONV_W - 1) * CT
        prow = sb("prow", [N_PRM, P])
        prm = sb("prm", [P, N_PRM])
        w_lr = sb("w_lr", [P, DEPTH, KT, RANK])
        w_a2 = sb("w_a2", [RANK, DEPTH, HEADS * DK])
        w_rt = sb("w_rt", [P, KT, E])
        u_mem = sb("u_mem", [P, CT * (T + 2 * (CONV_W - 1))])
        u_ext = u_mem[:, :].rearrange("p (t c) -> p t c", t=CT)
        sq = u_mem[:, 0:4 * T].rearrange("p (t c) -> p t c", t=4)
        more_no = sb("more_no", [P, MORE + 1, 2 * E])
        exp_no = sb("exp_no", [P, 2, E])
        rstd = sb("rstd", [P, T])

        o_mix_g, o_mix_b, o_ffn_g, o_ffn_b = (n * DEPTH * KT for n in range(4))
        o_ba = 4 * DEPTH * KT
        o_cw = o_ba + DEPTH * PAIRS
        o_gn = o_cw + DEPTH * CONV_W * CT
        o_cc = o_gn + DEPTH

        early = ExitStack()

        def sbe(name, shape, dt=F32):
            return early.enter_context(nc.sbuf_tensor(name, shape, dt))

        xh = sbe("xh", [P, KT, T], F32R)
        xl = sbe("xl", [P, KT, T], F32R)
        mix = ExitStack()

        def sbm(name, shape, dt=F32):
            return mix.enter_context(nc.sbuf_tensor(name, shape, dt))

        proj = sbm("proj", [P, 24, T])
        x_in = proj[:, :, :].rearrange("p a b -> p (a b)")[:, 0:TT * D].rearrange("p (t d) -> p t d", t=TT)
        lrT = sbm("lrT", [RANK, T])
        ga = sbm("ga", [P, PAIRS, T])
        og = sbm("og", [P, HEADS, T])
        gb = og[:, 0:PAIRS, :]
        gc = og[:, PAIRS:2 * PAIRS, :]
        kg = sbm("kg", [P, PAIRS, T])
        v_tok = sbm("v_tok", [P, TT, HEADS * DV])
        kd_tok = sbm("kd_tok", [P, TT * HEADS * DK])
        kd_t = kd_tok[:, :].rearrange("p (t c) -> p t c", t=TT)
        CVW = T + CONV_W - 1
        conv = [kd_tok[:, 0:2 * CVW].rearrange("p (a c) -> p a c", a=2),
                v_tok[:, 0:2, :].rearrange("p t c -> p (t c)")[:, 0:2 * CVW].rearrange("p (a c) -> p a c", a=2)]
        score = sbm("score", [P, TT, HEADS, P])
        given = sbm("given", [P, DEPTH, PAIRS, DV])
        S_NEW = LAST + 1
        state = sbm("state", [P, PAIRS, LAST + 2, DV])
        rows = sbm("rows", [P, 2, CONV_W - 1, CT])
        rowsT = sbm("rowsT", [2 * (CONV_W - 1) * CT, P])
        mix.close()
        over_proj = ExitStack()
        y_split = over_proj.enter_context(nc.sbuf_tensor("y_split", [P, 16, T], F32R))
        over_proj.close()
        dense = ExitStack()

        def sbd(name, shape, dt=F32):
            return dense.enter_context(nc.sbuf_tensor(name, shape, dt))

        silu_g = sbd("silu_g", [P, 2, T])
        hid = sbd("hid", [P, 2, T])
        hh = sbd("hh", [P, 4, T], F32R)
        hl = sbd("hl", [P, 4, T], F32R)
        dense.close()
        early.close()
        late = ExitStack()
        ctx.enter_context(late)

        def sbl(name, shape, dt=F32):
            return late.enter_context(nc.sbuf_tensor(name, shape, dt))

        xt_hi = sbl("xt_hi", [P, TT, D], F32R)
        xt_lo = sbl("xt_lo", [P, TT, D], F32R)
        xg = sbl("xg", [P, KT, 2, P], F32R)
        sg = sbl("sg", [P, 2, 512])
        hm = sbl("hm", [P, 2, 512])
        hT_hi = sbl("hT_hi", [P, 4, P], F32R)
        hT_lo = sbl("hT_lo", [P, 4, P], F32R)
        pick = sbl("pick", [P, TT, P], F32R)
        pickT = sbl("pickT", [P, T], F32R)
        g_col = sbl("g_col", [P, TT])
        g_slot = sbl("g_slot", [P, 2])
        ys = sbl("ys", [P, D])
        ys_hi = sbl("ys_hi", [P, D], F32R)
        ys_lo = sbl("ys_lo", [P, D], F32R)
        lg = sbl("lg", [P, TT, E])
        cmp_gt = sbl("cmp_gt", [P, TT, E, E])
        cmp_eq = sbl("cmp_eq", [P, TT, E, E])
        rank = sbl("rank", [P, TT, E])
        sel1 = sbl("sel1", [P, TT, E])
        sel2 = sbl("sel2", [P, TT, E])
        sel = sbl("sel", [P, TT, E])
        tmp_e = sbl("tmp_e", [P, TT, E])
        top = sbl("top", [P, 4, TT])
        gat = sbl("gat", [P, 2, TT])
        comb = sbl("comb", [P, TT, E])
        qpos = sbl("qpos", [P, TT, E])
        over = sbl("over", [P, 2, E])
        over_n = sbl("over_n", [P, 2 * E])
        over_i = sbl("over_i", [P, 2 * E])
        slot_of = sbl("slot_of", [P, MORE + 1, 2 * E])
        qsh = sbl("qsh", [P, TT, 2 * E])
        csh = sbl("csh", [P, TT, 2 * E])
        wide = sbl("wide", [P, TT * (MORE + 1), 2 * E])
        q_tab = sbl("q_tab", [P, TT, SLOTS])
        g_tab = sbl("g_tab", [P, TT, SLOTS])
        ctl_f = sbl("ctl_f", [P, 16])
        ctl = sbl("ctl", [1, 16], I32)
        y_tok = sbl("y_tok", [P, TT, D])

        ps = [ctx.enter_context(nc.psum_tensor(f"ps{b}", [P, 512], F32)) for b in range(8)]

        raw_landed = [sem(f"raw_landed{r}") for r in range(RAW)]
        hi_ready, lo_ready, unit_used = sem("hi_ready"), sem("lo_ready"), sem("unit_used")
        prm_landed, x_landed, small_landed, state_landed = (sem(n) for n in (
            "prm_landed", "x_landed", "small_landed", "state_landed"))
        const_step, const_ready = sem("const_step"), sem("const_ready")
        prm_turned, prm_ready, x_turned = sem("prm_turned"), sem("prm_ready"), sem("x_turned")
        x_ready, xh_ready, xl_ready = sem("x_ready"), sem("xh_ready"), sem("xl_ready")
        tile_done = sem("tile_done")
        sum_step, mean_done, centered, squared, var_part, ln_var, rstd_ready, scaled = (sem(n) for n in (
            "sum_step", "mean_done", "centered", "squared", "var_part", "ln_var", "rstd_ready", "scaled"))
        by_layer = lambda name: [sem(f"{name}{l}") for l in range(DEPTH)]
        proj_ready, lr_done, lr_ready, z_done, gate_act, gate_dve = (by_layer(n) for n in (
            "proj_ready", "lr_done", "lr_ready", "z_done", "gate_act", "gate_dve"))
        kd_turned, v_turned, kd_read, v_read, score_done, score_read = (by_layer(n) for n in (
            "kd_turned", "v_turned", "kd_read", "v_read", "score_done", "score_read"))
        ds_done, st_step, o_done, o_read, o_sq, ms_done, ms_act, og_step = (by_layer(n) for n in (
            "ds_done", "st_step", "o_done", "o_read", "o_sq", "ms_done", "ms_act", "og_step"))
        silu_done, cv_step, y_conv, rows_ready, rows_turned, rowsT_ready, yh_ready, yl_ready, r_ready = (
            by_layer(n) for n in ("silu_done", "cv_step", "y_conv", "rows_ready", "rows_turned", "rowsT_ready",
                                  "yh_ready", "yl_ready", "r_ready"))
        d_silu, d_hid, d_hh, d_hl, d_added = (sem(n) for n in ("d_silu", "d_hid", "d_hh", "d_hl", "d_added"))
        lg_done, xt_done, xth_ready, xtl_ready, rt_step, rt_exp, pos_done, ctl_ready = (sem(n) for n in (
            "lg_done", "xt_done", "xth_ready", "xtl_ready", "rt_step", "rt_exp", "pos_done",
            "ctl_ready"))
        x_scaled, pick_ready = sem("x_scaled"), sem("pick_ready")
        job_done, job_read, m_silu, m_hid, hT_hi_ready = (sem(n) for n in (
            "job_done", "job_read", "m_silu", "m_hid", "hT_hi_ready"))
        ys_ready, ys_hi_ready, ys_lo_ready = (sem(n) for n in ("ys_ready", "ys_hi_ready", "ys_lo_ready"))
        y_turned, y_ready_a, y_ready_v, y_stored, stored = (sem(n) for n in (
            "y_turned", "y_ready_a", "y_ready_v", "y_stored", "stored"))

        def slot(t, n, ring, a):
            return t[:, (n % ring) * UNIT:(n % ring + 1) * UNIT].rearrange("p (a c) -> p a c", a=a)

        def flat(t, n, ring):
            return t[:, (n % ring) * UNIT:(n % ring + 1) * UNIT]

        def upto(n, i, per):
            return n if i is None else i * per + n

        ST_STEPS = 1 + PAIRS * (NCH - 1)
        LAYER_STORES = 2 + 2 * PAIRS
        GD_Q, GD_KD = 7, 8
        TD_IN, TD_OUT = [0, 65], [12, 77]
        TD_FFN, TD_CHUNK = 16, 7
        UNITS_OUT = 4
        HALF_SUM = KT // 2 - 1
        SUMS = [KT, KT + HALF_SUM * FC, 2 * KT + HALF_SUM * FC]
        BUSY = {"x lands": 11, "first unit": 6, "mean": 4, "squares": 5, "norm": 17, "first gather": 24,
                "last scatter": 13}
        RT_LOGITS, RT_SEL, RT_DIFF = 4, 14, 19
        XT_ORDER = [1, 2, 3, 4, 5, 0]
        SMALL_LOADS = 3
        GATHERS = KT // 2
        TAIL_BANKS = [6, 7, 2, 3]
        Y_ORDER = [4, 5, 6, 7, 0, 1, 2, 3]

        def og_tile(k):
            if k >= CT:
                return og[:, k - CT, :]
            return proj[:, TCB[k // 2] + k % 2, :]

        def y_hi(k):
            return y_split[:, k - CT if k >= CT else 2 * CT + (k // 2) * 4 + k % 2, :]

        def y_lo(k):
            return y_split[:, k if k >= CT else 2 * CT + (k // 2) * 4 + 2 + k % 2, :]

        block = ctx.enter_context(nc.Block())

        @block.sync
        def _(sp):
            def load(n, src, a, i=None, per=0):
                if n >= RAW:
                    sp.wait_ge(lo_ready, upto(n - RAW + 1, i, per))
                sp.dma_start(slot(raw, n, RAW, a), src).then_inc(raw_landed[n % RAW], 16)

            def layer_units(l, between):
                for j, col in enumerate(IN_UNITS):
                    if j in between:
                        between[j]()
                    load(U_IN[l] + j, w_in[l, :, col:col + 256].rearrange("(k p) c -> p k c", p=P), KT)
                for j in range(4):
                    load(U_OUT[l] + j, w_out[l, :, 256 * j:256 * j + 256].rearrange("(k p) c -> p k c", p=P), KT)

            def parameters():
                row = 0
                for v, rows_of in ((ln_mix_g, "l (k p) -> (l k) p"), (ln_mix_b, "l (k p) -> (l k) p"),
                                   (ln_ffn_g, "l (k p) -> (l k) p"), (ln_ffn_b, "l (k p) -> (l k) p"),
                                   (b_alpha, "l (k p) -> (l k) p"), (conv_w, "l i (k p) -> (l i k) p"),
                                   (gla_norm_g, "l p -> l p"), (cache_conv, "l b r (k p) -> (l b r k) p")):
                    src = v if v is gla_norm_g else v.rearrange(rows_of, p=P)
                    sp.dma_start(prow[row:row + src.shape[0], :], src).then_inc(prm_landed, 16)
                    row += src.shape[0]
                sp.dma_start(w_lr[:], w_in[:, :, AL:AL + RANK].rearrange("l (k p) r -> p l k r", p=P)
                              ).then_inc(small_landed, 16)
                sp.dma_start(w_a2[:], w_alpha2.rearrange("l r c -> r l c")).then_inc(small_landed, 16)
                sp.dma_start(w_rt[:], moe_router[0].rearrange("(k p) e -> p k e", p=P)).then_inc(small_landed, 16)

            def given_states():
                for l in range(DEPTH):
                    for h in range(PAIRS):
                        sp.dma_start(given[:, l, h, :], state_gla[l, 0, 2 * h:2 * h + 2].rearrange(
                            "a k v -> (a k) v")).then_inc(state_landed, 16)

            for t in range(TT):
                src = x_prompt[0, P * t:P * t + P, :] if t < TT - 1 else x_sample[0]
                sp.dma_start(x_in[0:TOK[t], t, :], src).then_inc(x_landed, 16)
            layer_units(0, {2: parameters, RAW: given_states})
            with sp.Fori(0, FC) as c:
                for j in range(4):
                    w = (ffn_w_gate, ffn_w_up)[j % 2]
                    col = sp.snap(c * 512 + (j // 2) * 256)
                    load(U_FFN + j, w[0, :, bass.ds(col, 256)].rearrange("(k p) c -> p k c", p=P), KT, c, PER_CHUNK)
                for j in range(2):
                    row = sp.snap(c * 512)
                    load(U_FFN + 4 + j, ffn_w_down[0, bass.ds(row, 512), 512 * j:512 * j + 512].rearrange(
                        "(k p) c -> p k c", p=P), 4, c, PER_CHUNK)
            layer_units(1, {})

            def item_units(i, e):
                for j, (part, c, half) in enumerate(UNITS):
                    if part == "down":
                        src = moe_w_down[0, bass.ds(e, 1), 512 * c + 256 * half:512 * c + 256 * half + 256, :].rearrange(
                            "e (k p) d -> p (e k) d", p=P)
                        load(U_MOE + j, src, 2, i, PER_ITEM)
                    else:
                        w = moe_w_gate if part == "gate" else moe_w_up
                        src = w[0, bass.ds(e, 1), 512 * half:512 * half + 512, 512 * c:512 * c + 512].rearrange(
                            "e (k p) d -> p (e k) d", p=P)
                        load(U_MOE + j, src, 4, i, PER_ITEM)

            with sp.Fori(0, E) as i:
                item_units(i, i)
            sp.wait_ge(ctl_ready, 1)
            items = sp.value_load(ctl[0:1, MORE + 1:MORE + 2], min_val=E, max_val=E + MORE)
            with sp.If(items > E):
                with sp.Fori(E, items) as i:
                    e = sp.value_load(ctl[0:1, bass.ds(i - E, 1)], min_val=0, max_val=E - 1)
                    item_units(i, e)
            for j in range(AHEAD):
                n = U_MOE + j
                sp.wait_ge(lo_ready, items * PER_ITEM + (n - RAW + 1))
                sp.dma_start(slot(raw, n, RAW, 4), moe_w_gate[0, 0, 0:512, 0:512].rearrange(
                    "(k p) c -> p k c", p=P)).then_inc(raw_landed[n % RAW], 16)
            for half, ready in enumerate((y_ready_a, y_ready_v)):
                cols = slice(D // 2 * half, D // 2 * half + D // 2)
                for t in range(TT):
                    sp.wait_ge(ready, t + 1)
                    dst = y_prompt[0, P * t:P * t + P, cols] if t < TT - 1 else y_sample[0, :, cols]
                    sp.dma_start(dst, y_tok[0:TOK[t], t, cols]).then_inc(y_stored, 16)
            sp.wait_ge(y_stored, 16 * 2 * TT)

        @block.gpsimd
        def _(pool):
            done = 0

            def const(ins):
                nonlocal done
                done += 1
                ins.then_inc(const_step, 1)
                pool.wait_ge(const_step, done)

            const(pool.memset(ident[:], 0.0))
            const(pool.affine_select(out=ident[:], in_=ident[:], compare_op=ALU.not_equal, fill=1.0, base=0,
                                     pattern=[[-1, P]], channel_multiplier=1))
            const(pool.memset(mean_d[:], 1.0 / D))
            const(pool.memset(mean_v[:], 1.0 / DV))
            const(pool.memset(ones[:], 1.0))
            const(pool.memset(cst[:, 0:1], LN_EPS))
            const(pool.memset(cst[:, 1:2], 1.0))
            const(pool.memset(keep[:], 1.0))
            const(pool.memset(keep[:].rearrange("p (c t) -> p c t", t=CHUNK)[:, :, 0:1], 0.0))
            const(pool.affine_select(out=before[:], in_=ones[:], compare_op=ALU.is_gt, fill=0.0, base=0,
                                     pattern=[[1, P]], channel_multiplier=-1))
            const(pool.memset(lower_e[:], 1.0))
            const(pool.affine_select(out=lower_e[:], in_=lower_e[:], compare_op=ALU.is_gt, fill=0.0, base=0,
                                     pattern=[[1, E], [-1, E]], channel_multiplier=0))
            const(pool.iota(more_no[:], pattern=[[1, MORE + 1], [0, 2 * E]], base=E, channel_multiplier=0,
                            allow_small_or_imprecise_dtypes=True))
            const(pool.iota(exp_no[:], pattern=[[0, 2], [1, E]], base=0, channel_multiplier=0,
                            allow_small_or_imprecise_dtypes=True))
            const(pool.iota(slot_no[:], pattern=[[1, P]], base=1, channel_multiplier=0,
                            allow_small_or_imprecise_dtypes=True))
            const(pool.memset(causal[:], 1))
            const(pool.affine_select(out=causal[:], in_=causal[:], compare_op=ALU.is_ge, fill=0.0, base=0,
                                     pattern=[[1, P]], channel_multiplier=-1))
            const(pool.memset(causal[0:CHUNK, CHUNK:P], 0))
            pool.memset(v_tok[CHUNK:P, TT - 1, :], 0.0).then_inc(const_ready, 1)

            def add_bias(stage, o_b, scale):
                for k in range(KT):
                    pool.wait_ge(xl_ready, KT * (stage + 1) + k + 1)
                    at = o_b + KT * (stage // 2) + k
                    pool.tensor_scalar(x[:, k, :], x[:, k, :], prm[:, at:at + 1], scale, ALU.add, ALU.mult
                                       ).then_inc(x_ready, 1)

            def store(dst, src):
                pool.dma_start(dst, src).then_inc(stored, 16)

            for l in range(DEPTH):
                pool.wait_ge(rowsT_ready[l], 1)
                n = (CONV_W - 1) * CT
                store(cache_prompt[l, 0].rearrange("r (t p) -> (r t) p", p=P), rowsT[0:n, :])
                store(cache_sample[l, 0].rearrange("r (t p) -> (r t) p", p=P), rowsT[n:2 * n, :])
                pool.wait_ge(st_step[l], ST_STEPS)
                for h in range(PAIRS):
                    store(state_prompt[l, 0, 2 * h:2 * h + 2].rearrange("a k v -> (a k) v"), state[:, h, LAST, :])
                    store(state_sample[l, 0, 2 * h:2 * h + 2].rearrange("a k v -> (a k) v"), state[:, h, S_NEW, :])
                if l == 0:
                    add_bias(0, o_mix_b, ALPHA)
                    with pool.Fori(0, FC) as c:
                        for k in range(1, KT // 2):
                            pool.wait_ge(d_added, upto(KT + k + 1, c, KT))
                            pool.wait_ge(sum_step, upto(SUMS[0] + k - 1, c, HALF_SUM))
                            pool.tensor_tensor(rstd[:], x[:, 0, :] if k == 1 else rstd[:], x[:, k, :], ALU.add
                                               ).then_inc(sum_step, 1)
                    add_bias(1, o_ffn_b, 1.0)
            pool.wait_ge(stored, 16 * LAYER_STORES * DEPTH)


        @block.tensor
        def _(pe):
            def split_product(out, pairs, start, stop):
                for j, (wh, wl, hi, lo) in enumerate(pairs):
                    pe.matmul(out, wh, hi, start=start and j == 0, stop=False)
                    pe.matmul(out, wh, lo, start=False, stop=False)
                    mm = pe.matmul(out, wl, hi, start=False, stop=stop and j == len(pairs) - 1)
                return mm

            def two_tiles(n, wait_input, order=range(KT), hi=None, lo=None):
                for j, k in enumerate(order):
                    wait_input(j)
                    for half in range(2):
                        cols = slice(P * half, P * half + P)
                        pair = (slot(whi, n, SPLIT, KT)[:, k, cols], slot(wlo, n, SPLIT, KT)[:, k, cols],
                                hi(k) if hi else x_hi(k), lo(k) if lo else x_lo(k))
                        mm = split_product(ps[half][:, 0:T], [pair], j == 0, j == KT - 1)
                        if j == KT - 1:
                            mm.then_inc(unit_used if half else tile_done, 1)

            def x_hi(k):
                return xh[:, k, :]

            def x_lo(k):
                return xl[:, k, :]

            def by_tile(n, a, half, hi=x_hi, lo=x_lo):
                cols = slice(P * half, P * half + P)
                return [(slot(whi, n, SPLIT, a)[:, k, cols], slot(wlo, n, SPLIT, a)[:, k, cols],
                         hi(k), lo(k)) for k in range(KT)]

            def keep_busy(n, bank=ps[7]):
                for _ in range(n):
                    pe.matmul(bank[:, 0:P], mean_d[:], mean_d[:], start=True, stop=True)

            pe.wait_ge(const_step, 3)
            keep_busy(BUSY["x lands"])
            pe.wait_ge(x_landed, 16 * TT)
            for k in range(KT):
                if k >= 4:
                    pe.wait_ge(x_ready, k - 3)
                for t in range(TT):
                    mm = pe.transpose(ps[4 + k % 4][:, P * t:P * t + TOK[t]],
                                      x_in[0:TOK[t], t, P * k:P * k + P], ident[0:TOK[t], 0:TOK[t]])
                mm.then_inc(x_turned, 1)
            pe.wait_ge(prm_landed, 16 * 8)
            pe.transpose(ps[3][:, 0:N_PRM], prow[:, :], ident[0:N_PRM, 0:N_PRM]).then_inc(prm_turned, 1)
            pe.wait_ge(const_ready, 1)
            pe.wait_ge(x_ready, KT)
            keep_busy(BUSY["first unit"])

            def part_of_mean(stage, k, wait_residual):
                wait_residual(k)
                mm = pe.matmul(ps[4][:, 0:T], mean_d[:], x[:, k, :], start=k == 0, stop=k == KT - 1)
                if k == KT - 1:
                    mm.then_inc(mean_done, 1)

            def norm(stage, sums=None, wait_residual=None):
                idle = ps[0 if stage == 3 else 7]
                if sums:
                    keep_busy(BUSY["mean"], idle)
                    pe.wait_ge(sum_step, sums)
                    mm = pe.matmul(ps[4][:, 0:T], mean_d[:], rstd[:], start=True, stop=not wait_residual)
                if wait_residual:
                    for k in range(KT // 2, KT):
                        part_of_mean(stage, k, wait_residual)
                elif sums:
                    mm.then_inc(mean_done, 1)
                keep_busy(BUSY["squares"], idle)
                for k in range(KT):
                    pe.wait_ge(squared, KT * stage + k + 1)
                    pe.matmul(ps[5][:, 0:T], mean_d[:], sq[:, k % 4, :], start=k == 0, stop=k == KT - 1
                              ).then_inc(var_part, 1)
                keep_busy(BUSY["norm"], idle)

            def mixer(l):
                def gates():
                    pe.wait_ge(lr_ready[l], 1)
                    for h in range(PAIRS):
                        pe.matmul(ps[5 + h][:, 0:T], w_a2[:, l, P * h:P * h + P], lrT[:, :],
                                  start=True, stop=True).then_inc(z_done[l], 1)

                def turn_kv():
                    pe.wait_ge(gate_dve[l], GD_KD)
                    for t in range(TT):
                        for h in range(PAIRS):
                            at = (t % 2) * 256 + P * h
                            mm = pe.transpose(ps[4 + t // 2][0:TOK[t], at:at + P],
                                              proj[:, TK + h, P * t:P * t + TOK[t]], ident[:])
                        if t >= TT - 2:
                            mm.then_inc(kd_turned[l], 1)
                    pe.wait_ge(proj_ready[l], TV + VT)
                    for t in range(2):
                        for h in range(VT):
                            mm = pe.transpose(ps[6 + t][:, P * h:P * h + P], proj[:, TV + h, P * t:P * t + P],
                                              ident[:])
                        mm.then_inc(v_turned[l], 1)

                def scores():
                    pe.wait_ge(v_read[l], 1)
                    for h in range(VT):
                        mm = pe.transpose(ps[6][0:DEC, P * h:P * h + P], proj[:, TV + h, 2 * P:T], ident[:])
                    mm.then_inc(v_turned[l], 1)
                    pe.wait_ge(kd_read[l], 2)
                    for par in range(2):
                        r = slice(DK * par, DK * par + DK)
                        for n, (t, h) in enumerate((t, h) for t in range(2) for h in range(par, HEADS, 2)):
                            mm = pe.matmul(ps[4 + par][:, P * n:P * n + P], kg[r, h // 2, P * t:P * t + P],
                                           proj[r, TQ + h // 2, P * t:P * t + P], start=True, stop=True)
                        mm.then_inc(score_done[l], 1)

                def chunk_state(c, bank, at):
                    r = slice(CHUNK * (c % 2), CHUNK * (c % 2) + CHUNK)
                    for h in range(HEADS):
                        o = slice(DK * (h % 2), DK * (h % 2) + DK)
                        col = at + DV * (h // 2)
                        mm = pe.matmul(bank[o, col:col + DV], kd_t[r, c // 2, DK * h:DK * h + DK],
                                       v_tok[r, c // 2, DV * h:DV * h + DV], start=True, stop=True)
                    return mm

                def states():
                    for par in range(2):
                        pe.wait_ge(score_read[l], par + 1)
                        r = slice(DK * par, DK * par + DK)
                        for n, h in enumerate(range(par, HEADS, 2)):
                            mm = pe.matmul(ps[4 + par][0:DEC, CHUNK * n:CHUNK * n + CHUNK], kg[r, h // 2, 2 * P:T],
                                           proj[r, TQ + h // 2, 2 * P:T], start=True, stop=True)
                        mm.then_inc(score_done[l], 1)
                    pe.wait_ge(v_read[l], 3)
                    for par in range(2):
                        for c in range(par, LAST, 2):
                            mm = chunk_state(c, ps[6 + par], (c // 2) * 256)
                        mm.then_inc(ds_done[l], 1)
                    pe.wait_ge(score_read[l], 3)
                    chunk_state(LAST, ps[4], 0).then_inc(ds_done[l], 1)

                def outputs():
                    pe.wait_ge(st_step[l], ST_STEPS)
                    pe.wait_ge(score_read[l], 4)
                    for h in range(HEADS):
                        r = slice(DK * (h % 2), DK * (h % 2) + DK)
                        for c in range(NCH):
                            cols = slice(CHUNK * c, CHUNK * c + CHUNK)
                            inner = slice(CHUNK * (c % 2), CHUNK * (c % 2) + CHUNK)
                            lone = c == 0
                            mm = pe.matmul(ps[4 + h][:, cols], v_tok[:, c // 2, DV * h:DV * h + DV],
                                           score[:, c // 2, h, inner], start=True, stop=lone)
                            if not lone:
                                s = given[r, l, h // 2, :] if c == LAST else state[r, h // 2, c, :]
                                mm = pe.matmul(ps[4 + h][:, cols], s, proj[r, TQ + h // 2, cols],
                                               start=False, stop=True)
                        mm.then_inc(o_done[l], 1)

                def mean_squares():
                    for h in range(HEADS):
                        pe.wait_ge(o_sq[l], h + 1)
                        pe.matmul(ps[4 + h][:, 0:T], mean_v[:], proj[:, h, :], start=True, stop=True
                                  ).then_inc(ms_done[l], 1)

                hooks = {1: gates, 5: turn_kv, 6: scores, 7: states, 8: outputs, 9: mean_squares}
                pe.wait_ge(lo_ready, U_IN[l] + 1)
                two_tiles(U_IN[l], lambda j: pe.wait_ge(xl_ready, KT * 2 * l + j + 1))
                pe.wait_ge(x_ready, KT * (1 + 2 * l))
                pe.wait_ge(small_landed, 16 * SMALL_LOADS)
                for k in range(KT):
                    mm = pe.matmul(ps[4][0:RANK, 0:T], w_lr[:, l, k, :], x[:, k, :], start=k == 0, stop=k == KT - 1)
                mm.then_inc(lr_done[l], 1)
                if l == 0:
                    pe.wait_ge(prm_ready, 1)
                for u in range(1, 12):
                    n = U_IN[l] + u
                    pe.wait_ge(lo_ready, n + 1)
                    for half in range(2):
                        if 2 * u + half >= 4:
                            pe.wait_ge(proj_ready[l], 2 * u + half - 3)
                        mm = split_product(ps[(2 * u + half) % 4][:, 0:T], by_tile(n, KT, half), True, True)
                        mm.then_inc(unit_used if half else tile_done, 1)
                    if u in hooks:
                        hooks[u]()
                for u in range(UNITS_OUT):
                    n = U_OUT[l] + u
                    pe.wait_ge(lo_ready, n + 1)
                    if u == 0:
                        two_tiles(n, lambda j: pe.wait_ge(yl_ready[l], j + 1), Y_ORDER, y_hi, y_lo)
                        continue
                    for half in range(2):
                        m = 2 * u + half
                        if m >= 4:
                            pe.wait_ge(r_ready[l], m - 3)
                        mm = split_product(ps[m % 4][:, 0:T], by_tile(n, KT, half, y_hi, y_lo), True, True)
                        mm.then_inc(unit_used if half else tile_done, 1)
                pe.wait_ge(rows_ready[l], 1)
                pe.transpose(ps[6][0:2 * (CONV_W - 1) * CT, 0:P], rows[:, :, :, :].rearrange("p a b c -> p (a b c)"),
                             ident[:]).then_inc(rows_turned[l], 1)
                norm(2 * l, SUMS[2 * l])

            def dense_mixer():
                with pe.Fori(0, FC) as c:
                    for j in range(4):
                        n, q = U_FFN + j, j // 2
                        pe.wait_ge(lo_ready, upto(n + 1, c, PER_CHUNK))
                        if j == 0:
                            pe.wait_ge(d_added, upto(4 + 2, c, 8))
                            two_tiles(n, lambda k: pe.wait_ge(xl_ready, KT + k + 1))
                            continue
                        for half in range(2):
                            bank = 2 * (j % 2) + half
                            if q == 0:
                                pe.wait_ge(d_added, upto(4 + bank + 1, c, 8))
                            else:
                                pe.wait_ge(d_hid, upto(half + 1, c, 4))
                            mm = split_product(ps[bank][:, 0:T], by_tile(n, KT, half), True, True)
                            mm.then_inc(unit_used if half else tile_done, 1)
                    n = U_FFN + 4
                    pe.wait_ge(lo_ready, upto(n + 1, c, PER_CHUNK))
                    pe.wait_ge(d_added, upto(4, c, 8))
                    for k in range(4):
                        pe.wait_ge(d_hl, upto(k + 1, c, 4))
                        for m in range(4):
                            wh, wl = (slot(w, n, SPLIT, 4)[:, k, P * m:P * m + P] for w in (whi, wlo))
                            mm = split_product(ps[4 + m][:, 0:T], [(wh, wl, hh[:, k, :], hl[:, k, :])], k == 0, k == 3)
                    mm.then_inc(unit_used, 1)
                    n = U_FFN + 5
                    pe.wait_ge(lo_ready, upto(n + 1, c, PER_CHUNK))
                    for m in range(4):
                        pairs = [(slot(whi, n, SPLIT, 4)[:, k, P * m:P * m + P],
                                  slot(wlo, n, SPLIT, 4)[:, k, P * m:P * m + P], hh[:, k, :], hl[:, k, :])
                                 for k in range(4)]
                        split_product(ps[m][:, 0:T], pairs, True, True).then_inc(unit_used if m == 3 else tile_done, 1)
                pe.wait_ge(d_added, 8 * FC + 4)
                norm(1, SUMS[1], lambda k: pe.wait_ge(d_added, 8 * FC + k + 1))

            def router():
                for k in range(KT):
                    pe.wait_ge(x_ready, 3 * KT + k + 1)
                    for t in range(TT):
                        mm = pe.matmul(ps[t][0:TOK[t], 0:E], x[:, k, P * t:P * t + TOK[t]],
                                       w_rt[:, k, :], start=k == 0, stop=k == KT - 1)
                mm.then_inc(lg_done, 1)
                for j in XT_ORDER:
                    t, half = j // 2, j % 2
                    if j == 0:
                        pe.wait_ge(rt_step, RT_LOGITS)
                    for k in range(4):
                        mm = pe.transpose(ps[2 + j][0:TOK[t], P * k:P * k + P],
                                          x[:, 4 * half + k, P * t:P * t + TOK[t]], ident[:])
                    mm.then_inc(xt_done, 1)
                pe.wait_ge(rt_step, RT_SEL)
                sel_by = lambda a, b: sel[:, a:b, :].rearrange("p t e -> p (t e)")
                pe.matmul(ps[1][:, 0:E * TT], before[:], sel_by(0, TT), start=True, stop=False)
                for t in range(1, TT):
                    pe.matmul(ps[1][:, E * t:E * TT], ones[:], sel_by(0, TT - t), start=False, stop=t == TT - 1)
                for t in range(TT):
                    mm = pe.matmul(ps[1][:, E * TT:E * TT + E], ones[:], sel_by(t, t + 1), start=t == 0, stop=t == TT - 1)
                mm.then_inc(pos_done, 1)
                keep_busy(BUSY["first gather"], ps[0])
                pe.wait_ge(xtl_ready, 2 * TT)
                pe.wait_ge(pick_ready, 1)
                for g in range(GATHERS):
                    if g >= 2:
                        pe.wait_ge(job_read, g - 1)
                    gather(g, ps[6 + g % 2])

            def gather(g, bank):
                for kk in range(2):
                    k = 2 * g + kk
                    for n, xt in enumerate((xt_hi, xt_lo)):
                        at = (2 * kk + n) * P
                        for t in range(TT):
                            mm = pe.matmul(bank[:, at:at + P], xt[:, t, P * k:P * k + P], pick[:, t, :],
                                           start=t == 0, stop=t == TT - 1)
                mm.then_inc(job_done, 1)

            def scatter(k, bank):
                pe.matmul(bank[:, 0:T], ys_hi[:, P * k:P * k + P], pickT[:, :], start=True, stop=False)
                pe.matmul(bank[:, 0:T], ys_lo[:, P * k:P * k + P], pickT[:, :], start=False, stop=True
                          ).then_inc(job_done, 1)

            def experts(items):
                with pe.Fori(0, items) as i:
                    unit, job = 0, GATHERS
                    for part, c, half in ITEM:
                        if part in ("gate", "up"):
                            n = U_MOE + unit
                            unit += 1
                            if half == 0 and part == "gate":
                                if c == 0:
                                    pe.wait_ge(job_read, upto(GATHERS, i, PER_JOBS))
                                pe.wait_ge(m_hid, upto(max(0, c - 1), i, FC))
                            bank = ps[2 * (c % 2) + (part == "up")]
                            pe.wait_ge(lo_ready, upto(n + 1, i, PER_ITEM))
                            for j in range(4):
                                k = 4 * half + j
                                wh, wl = slot(whi, n, SPLIT, 4)[:, j, :], slot(wlo, n, SPLIT, 4)[:, j, :]
                                pe.matmul(bank[:], xg[:, k, 0, :], wh, start=k == 0, stop=False)
                                pe.matmul(bank[:], xg[:, k, 0, :], wl, start=False, stop=False)
                                mm = pe.matmul(bank[:], xg[:, k, 1, :], wh, start=False, stop=k == KT - 1)
                            mm.then_inc(unit_used, 1)
                        elif part == "down":
                            n = U_MOE + unit
                            unit += 1
                            if half == 0:
                                pe.wait_ge(job_read, upto(turned[c], i, PER_JOBS))
                                if c == 0:
                                    pe.wait_ge(ys_ready, upto(0, i, 2))
                            pe.wait_ge(lo_ready, upto(n + 1, i, PER_ITEM))
                            for j in range(2):
                                k = 2 * half + j
                                for hT, ws in ((hT_hi, (whi, wlo)), (hT_lo, (whi,))):
                                    for w in ws:
                                        for d in range(2):
                                            mm = pe.matmul(ps[4 + d][:], hT[:, k, :],
                                                           slot(w, n, SPLIT, 2)[:, j, 512 * d:512 * d + 512],
                                                           start=c == 0 and k == 0 and hT is hT_hi and w is whi,
                                                           stop=c == FC - 1 and k == 3 and hT is hT_lo)
                            mm.then_inc(unit_used, 1)
                        else:
                            bank = ps[6 + job % 2]
                            pe.wait_ge(job_read, upto(job - 1, i, PER_JOBS))
                            job += 1
                            if part == "T":
                                turned[c] = job
                                pe.wait_ge(m_hid, upto(c + 1, i, FC))
                                for f in range(4):
                                    mm = pe.transpose(bank[:, P * f:P * f + P], hm[:, c % 2, P * f:P * f + P], ident[:])
                                mm.then_inc(job_done, 1)
                            elif part == "S":
                                if c in (0, KT // 2):
                                    pe.wait_ge(ys_lo_ready, upto(1 if c == 0 else 2, i, 2))
                                scatter(c, bank)
                            elif part == "GT":
                                for t in range(TT):
                                    pe.transpose(bank[:, P * t:P * t + TOK[t]], pick[0:TOK[t], t, :].bitcast(F32),
                                                 ident[0:TOK[t], 0:TOK[t]])
                                for t in range(TT):
                                    mm = pe.matmul(bank[:, T:T + 1], pick[:, t, :].bitcast(F32), g_col[:, t:t + 1],
                                                   start=t == 0, stop=t == TT - 1)
                                mm.then_inc(job_done, 1)
                            else:
                                if c == 0:
                                    pe.wait_ge(pick_ready, upto(2, i, 1))
                                gather(c, bank)
                keep_busy(BUSY["last scatter"], ps[0])
                for k in range(KT):
                    if k % (KT // 2) == 0:
                        pe.wait_ge(ys_lo_ready, items * 2 + (2 * k // KT + 1))
                    if k >= 4:
                        pe.wait_ge(job_read, items * PER_JOBS + (GATHERS + k - 3))
                    elif k == 0:
                        pe.wait_ge(job_read, items * PER_JOBS + GATHERS)
                    scatter(k, ps[TAIL_BANKS[k % 4]])
                    if k >= 2:
                        part_of_mean(3, k - 2, lambda k: pe.wait_ge(job_read, items * PER_JOBS + (GATHERS + k + 1)))
                for k in range(KT - 2, KT):
                    part_of_mean(3, k, lambda k: pe.wait_ge(job_read, items * PER_JOBS + (GATHERS + k + 1)))
                norm(3)

            turned = {}
            mixer(0)
            dense_mixer()
            mixer(1)
            router()
            pe.wait_ge(ctl_ready, 1)
            items = pe.value_load(ctl[0:1, MORE + 1:MORE + 2], min_val=E, max_val=E + MORE)
            experts(items)
            for half in range(2):
                pe.wait_ge(x_ready, 4 * KT + 4 * half + 4)
                for t in range(TT):
                    for k in range(4):
                        mm = pe.transpose(ps[half + 2 * (t % 2) if t < 2 else 6 + half][0:TOK[t], P * k:P * k + P],
                                          x[:, 4 * half + k, P * t:P * t + TOK[t]], ident[:])
                    mm.then_inc(y_turned, 1)

        @block.scalar
        def _(act):
            def round_unit(n, i=None, per=0):
                act.wait_ge(raw_landed[n % RAW], upto(16 * (n // RAW + 1), i, 16 * (per // RAW)))
                if n >= SPLIT:
                    act.wait_ge(unit_used, upto(n - SPLIT + 1, i, per))
                act.activation(flat(whi, n, SPLIT), flat(raw, n, RAW), ACT.Copy).then_inc(hi_ready, 1)

            def per_column(v, n):
                return prm[:, v + n:v + n + 1]

            for k in range(KT):
                act.wait_ge(x_ready, k + 1)
                act.activation(xh[:, k, :], x[:, k, :], ACT.Copy).then_inc(xh_ready, 1)
                if k == 3:
                    round_unit(0)
            round_unit(1)
            act.wait_ge(prm_turned, 1)
            act.activation(prm[:], ps[3][:, 0:N_PRM], ACT.Copy).then_inc(prm_ready, 1)
            act.wait_ge(prm_ready, 1)

            def norm(stage, o_b, split):
                act.preload_act_table(ACT.Ln)
                for k in range(KT):
                    act.wait_ge(centered, KT * stage + k + 1)
                    if KT * stage + k >= 4:
                        act.wait_ge(var_part, KT * stage + k - 3)
                    act.activation(sq[:, k % 4, :], x[:, k, :], ACT.Square).then_inc(squared, 1)
                act.wait_ge(var_part, KT * stage + KT)
                act.activation(rstd[:], ps[5][:, 0:T], ACT.Ln, bias=cst[:, 0:1]).then_inc(ln_var, 1)
                act.wait_ge(ln_var, stage + 1)
                act.activation(rstd[:], rstd[:], ACT.Exp, scale=-0.5).then_inc(rstd_ready, 1)
                if split:
                    for k in range(KT):
                        act.wait_ge(scaled, KT * stage + k + 1)
                        act.activation(xh[:, k, :], x[:, k, :], ACT.Identity,
                                       bias=per_column(o_b, KT * (stage // 2) + k)).then_inc(xh_ready, 1)
                    return
                for k in range(KT):
                    act.wait_ge(scaled, KT * stage + k + 1)
                    act.activation(x[:, k, :], x[:, k, :], ACT.Identity, bias=per_column(o_b, KT * (stage // 2) + k)
                                   ).then_inc(x_ready, 1)

            def mixer(l):
                def low_rank():
                    act.wait_ge(lr_done[l], 1)
                    act.activation(lrT[:], ps[4][0:RANK, 0:T], ACT.Copy).then_inc(lr_ready[l], 1)

                def z():
                    for h in range(PAIRS):
                        act.wait_ge(z_done[l], h + 1)
                        act.activation(ga[:, h, :], ps[5 + h][:, 0:T], ACT.Identity,
                                       bias=per_column(o_ba, PAIRS * l + h)).then_inc(gate_act[l], 1)

                def softplus():
                    act.wait_ge(gate_dve[l], 1)
                    act.activation(gc, gc, ACT.Exp, scale=-1.0).then_inc(gate_act[l], 1)
                    act.wait_ge(gate_act[l], 3)
                    act.activation(gc, gc, ACT.Ln, bias=cst[:, 1:2]).then_inc(gate_act[l], 1)

                def exps():
                    act.wait_ge(gate_dve[l], 4)
                    act.activation(ga[:], gb, ACT.Exp, scale=1.0 / GATE_TEMP).then_inc(gate_act[l], 1)
                    act.activation(gc, gb, ACT.Exp, scale=-1.0 / GATE_TEMP).then_inc(gate_act[l], 1)

                def exp_rest():
                    act.wait_ge(gate_dve[l], 7)
                    act.activation(gc, gc, ACT.Exp, scale=1.0 / GATE_TEMP).then_inc(gate_act[l], 1)

                def read_v():
                    for t in range(2):
                        act.wait_ge(v_turned[l], t + 1)
                        act.activation(v_tok[:, t, :], ps[6 + t][:], ACT.Copy).then_inc(v_read[l], 1)

                def read_v_sample():
                    act.wait_ge(v_turned[l], 3)
                    act.activation(v_tok[0:DEC, TT - 1, :], ps[6][0:DEC, :], ACT.Copy).then_inc(v_read[l], 1)

                def silu():
                    act.wait_ge(proj_ready[l], TG + VT)
                    act.activation(proj[:, TG:TG + VT, :], proj[:, TG:TG + VT, :], ACT.Silu).then_inc(silu_done[l], 1)

                def squares():
                    act.preload_act_table(ACT.Ln)
                    act.wait_ge(o_done[l], HEADS)
                    for h in range(HEADS):
                        act.wait_ge(o_read[l], h + 1)
                        act.activation(proj[:, h, :], og[:, h, :], ACT.Square).then_inc(o_sq[l], 1)

                def rms():
                    for h in range(HEADS):
                        act.wait_ge(ms_done[l], h + 1)
                        act.activation(proj[:, TV + h, :], ps[4 + h][:, 0:T], ACT.Ln, bias=cst[:, 0:1]
                                       ).then_inc(ms_act[l], 1)
                    for h in range(HEADS):
                        act.wait_ge(ms_act[l], h + 1)
                        act.activation(proj[:, TV + h, :], proj[:, TV + h, :], ACT.Exp, scale=-0.5
                                       ).then_inc(ms_act[l], 1)

                def round_y(order):
                    def run():
                        for k in order:
                            if k >= CT:
                                act.wait_ge(og_step[l], 2 * (k - CT) + 2)
                            else:
                                act.wait_ge(y_conv[l], k + 1)
                            act.activation(y_hi(k), og_tile(k), ACT.Copy).then_inc(yh_ready[l], 1)
                    return run

                hooks = {0: [low_rank], 1: [z], 2: [softplus, exps], 3: [exp_rest], 5: [read_v], 6: [read_v_sample],
                         7: [silu], 8: [squares], 9: [rms],
                         10: [round_y(Y_ORDER[:6])], 11: [round_y(Y_ORDER[6:])]}
                for u in range(12):
                    n = U_IN[l] + u
                    if u < 11:
                        round_unit(n + AHEAD)
                    for half in range(2):
                        if half:
                            act.wait_ge(unit_used, n + 1)
                        else:
                            act.wait_ge(tile_done, TD_IN[l] + u + 1)
                        act.activation(proj[:, 2 * u + half, :], ps[(2 * u + half) % 4][:, 0:T], ACT.Copy
                                       ).then_inc(proj_ready[l], 1)
                    if u == 11:
                        round_unit(n + AHEAD)
                    for hook in hooks.get(u, []):
                        hook()
                for u in range(UNITS_OUT):
                    round_unit(U_OUT[l] + u + AHEAD)
                act.wait_ge(rows_turned[l], 1)
                if l:
                    act.wait_ge(stored, 16 * LAYER_STORES * l)
                act.activation(rowsT[:], ps[6][0:2 * (CONV_W - 1) * CT, 0:P], ACT.Copy).then_inc(rowsT_ready[l], 1)
                norm(2 * l, o_mix_b, l == 0)

            def dense_mixer():
                act.preload_act_table(ACT.Silu)
                with act.Fori(0, FC) as c:
                    for j in range(PER_CHUNK):
                        round_unit(U_FFN + j + AHEAD, c, PER_CHUNK)
                        q = j // 2
                        if j in (0, 2):
                            act.wait_ge(d_hid, upto(2 * q, c, 4))
                            for half in range(2):
                                if half:
                                    act.wait_ge(unit_used, upto(U_FFN + j + 1, c, PER_CHUNK))
                                else:
                                    act.wait_ge(tile_done, upto(TD_FFN + j + 1, c, TD_CHUNK))
                                act.activation(silu_g[:, half, :], ps[half][:, 0:T], ACT.Silu).then_inc(d_silu, 1)
                        elif j in (1, 3):
                            for half in range(2):
                                act.wait_ge(d_hid, upto(2 * q + half + 1, c, 4))
                                act.activation(hh[:, 2 * q + half, :], hid[:, half, :], ACT.Copy).then_inc(d_hh, 1)
                norm(1, o_ffn_b, True)

            def router():
                for n, j in enumerate(XT_ORDER):
                    t, half = j // 2, j % 2
                    act.wait_ge(xt_done, n + 1)
                    act.activation(xt_hi[0:TOK[t], t, 512 * half:512 * half + 512], ps[2 + j][0:TOK[t], :],
                                   ACT.Copy).then_inc(xth_ready, 1)
                act.wait_ge(rt_step, RT_DIFF)
                act.activation(top[:, 3, :], top[:, 2, :], ACT.Exp).then_inc(rt_exp, 1)
                act.activation(x[:].rearrange("p k t -> p (k t)"), x[:].rearrange("p k t -> p (k t)"), ACT.Copy,
                               scale=ALPHA).then_inc(x_scaled, 1)
                act.preload_act_table(ACT.Silu)

            def experts(items):
                with act.Fori(0, items) as i:
                    unit, job = 0, GATHERS
                    for part, c, half in ITEM:
                        if part in ("gate", "up", "down"):
                            n = U_MOE + unit
                            unit += 1
                            round_unit(n + AHEAD, i, PER_ITEM)
                            if part == "gate" and half:
                                act.wait_ge(unit_used, upto(n + 1, i, PER_ITEM))
                                act.wait_ge(m_hid, upto(max(0, c - 1), i, FC))
                                act.activation(sg[:, c % 2, :], ps[2 * (c % 2)][:], ACT.Silu).then_inc(m_silu, 1)
                        else:
                            job += 1
                            if part == "T":
                                act.wait_ge(job_done, upto(job, i, PER_JOBS))
                                act.activation(hT_hi[:, :, :].rearrange("p f s -> p (f s)"), ps[6 + (job - 1) % 2][:],
                                               ACT.Copy).then_inc(hT_hi_ready, 1)
                            elif part == "GT":
                                slots_known = job
                    act.wait_ge(unit_used, upto(U_MOE + PER_ITEM, i, PER_ITEM))
                    act.wait_ge(job_read, upto(slots_known, i, PER_JOBS))
                    act.wait_ge(ys_lo_ready, upto(2, i, 2))
                    for d in range(2):
                        act.activation(ys[:, 512 * d:512 * d + 512], ps[4 + d][:], ACT.Copy, scale=g_slot[:, 0:1]
                                       ).then_inc(ys_ready, 1)
                    for d in range(2):
                        act.wait_ge(ys_ready, upto(d + 1, i, 2))
                        act.activation(ys_hi[:, 512 * d:512 * d + 512], ys[:, 512 * d:512 * d + 512], ACT.Copy
                                       ).then_inc(ys_hi_ready, 1)
                norm(3, o_ffn_b, False)

            mixer(0)
            dense_mixer()
            mixer(1)
            router()
            act.wait_ge(ctl_ready, 1)
            items = act.value_load(ctl[0:1, MORE + 1:MORE + 2], min_val=E, max_val=E + MORE)
            experts(items)
            for t in range(TT):
                act.wait_ge(y_turned, t + 1)
                act.activation(y_tok[0:TOK[t], t, 0:512], ps[2 * (t % 2) if t < 2 else 6][0:TOK[t], :], ACT.Copy
                               ).then_inc(y_ready_a, 1)

        @block.vector
        def _(dve):
            def rest_unit(n, i=None, per=0):
                dve.wait_ge(hi_ready, upto(n + 1, i, per))
                dve.tensor_tensor(flat(wlo, n, SPLIT), flat(raw, n, RAW), flat(whi, n, SPLIT).bitcast(F32),
                                  ALU.subtract).then_inc(lo_ready, 1)

            def per_column(v, n):
                return prm[:, v + n:v + n + 1]

            dve.memset(score[:], 0.0).then_inc(d_added, KT)

            def rest(k):
                dve.wait_ge(xh_ready, k + 1)
                dve.tensor_tensor(xl[:, k, :], x[:, k, :], xh[:, k, :].bitcast(F32), ALU.subtract).then_inc(xl_ready, 1)

            for k in range(KT):
                dve.wait_ge(x_turned, k + 1)
                dve.tensor_copy(x[:, k, :], ps[4 + k % 4][:, 0:T]).then_inc(x_ready, 1)
                if 1 <= k <= 4:
                    rest(k - 1)
            rest_unit(0)
            for k in range(4, KT):
                rest(k)
            rest_unit(1)
            dve.wait_ge(prm_ready, 1)

            def norm(stage, o_g, o_b, split, meanwhile=None):
                dve.wait_ge(mean_done, stage + 1)
                for k in range(KT):
                    dve.tensor_tensor(x[:, k, :], x[:, k, :], ps[4][:, 0:T], ALU.subtract).then_inc(centered, 1)
                if meanwhile:
                    meanwhile()
                dve.wait_ge(rstd_ready, stage + 1)

                def rest(k):
                    dve.wait_ge(xh_ready, KT * (stage + 1) + k + 1)
                    dve.scalar_tensor_tensor(out=xl[:, k, :], in0=x[:, k, :],
                                             scalar=per_column(o_b, KT * (stage // 2) + k),
                                             in1=xh[:, k, :].bitcast(F32), op0=ALU.add, op1=ALU.subtract
                                             ).then_inc(xl_ready, 1)

                for k in range(KT):
                    dve.wait_ge(squared, KT * stage + k + 1)
                    dve.scalar_tensor_tensor(out=x[:, k, :], in0=x[:, k, :],
                                             scalar=per_column(o_g, KT * (stage // 2) + k), in1=rstd[:],
                                             op0=ALU.mult, op1=ALU.mult).then_inc(scaled, 1)
                    if split and k:
                        rest(k - 1)
                if split:
                    rest(KT - 1)

            def mixer(l):
                def absolute():
                    dve.wait_ge(gate_act[l], PAIRS)
                    dve.scalar_tensor_tensor(out=gc, in0=ga[:], scalar=-1.0, in1=ga[:], op0=ALU.mult, op1=ALU.max
                                             ).then_inc(gate_dve[l], 1)

                def log_gates():
                    dve.wait_ge(gate_act[l], 4)
                    dve.scalar_tensor_tensor(out=ga[:], in0=ga[:], scalar=0.0, in1=gc, op0=ALU.min,
                                             op1=ALU.subtract).then_inc(gate_dve[l], 1)
                    dve.wait_ge(gate_dve[l], 2)
                    for h in range(PAIRS):
                        dve.tensor_tensor_scan(gb[:, h, :], keep[:], ga[:, h, :], 0.0, ALU.mult, ALU.add
                                               ).then_inc(gate_dve[l], 1)

                def gated_qk():
                    dve.wait_ge(gate_act[l], 6)
                    dve.wait_ge(proj_ready[l], TK + PAIRS)
                    q, k = proj[:, TQ:TQ + PAIRS, :], proj[:, TK:TK + PAIRS, :]
                    dve.scalar_tensor_tensor(out=q, in0=q, scalar=DK ** -0.5, in1=ga[:], op0=ALU.mult, op1=ALU.mult
                                             ).then_inc(gate_dve[l], 1)
                    dve.tensor_tensor(kg[:], k, gc, ALU.mult).then_inc(gate_dve[l], 1)
                    dve.wait_ge(gate_dve[l], 6)
                    b = gb.rearrange("p h (c t) -> p h c t", t=CHUNK)
                    dve.tensor_tensor(gc.rearrange("p h (c t) -> p h c t", t=CHUNK),
                                      b[:, :, :, CHUNK - 1:CHUNK].to_broadcast([P, PAIRS, NCH, CHUNK]), b,
                                      ALU.subtract).then_inc(gate_dve[l], 1)

                def kd():
                    dve.wait_ge(gate_act[l], 7)
                    k = proj[:, TK:TK + PAIRS, :]
                    dve.tensor_tensor(k, k, gc, ALU.mult).then_inc(gate_dve[l], 1)

                def read_kd():
                    dve.wait_ge(kd_turned[l], 1)
                    dve.tensor_copy(kd_tok[:, 0:512], ps[4][:]).then_inc(kd_read[l], 1)
                    dve.wait_ge(kd_turned[l], 2)
                    dve.tensor_copy(kd_tok[0:DEC, 512:768], ps[5][0:DEC, 0:256]).then_inc(kd_read[l], 1)

                def mask_scores():
                    for par in range(2):
                        dve.wait_ge(score_done[l], par + 1)
                        for t in range(2):
                            mm = dve.copy_predicated(
                                score[:, t, par::2, :], causal[:].unsqueeze(1).to_broadcast([P, 2, P]),
                                ps[4 + par][:, 256 * t:256 * t + 256].rearrange("p (h i) -> p h i", h=2))
                        mm.then_inc(score_read[l], 1)

                def state_chain():
                    for par in range(2):
                        dve.wait_ge(score_done[l], 3 + par)
                        dve.copy_predicated(
                            score[0:DEC, TT - 1, par::2, 0:CHUNK],
                            causal[0:DEC, 0:CHUNK].unsqueeze(1).to_broadcast([DEC, 2, CHUNK]),
                            ps[4 + par][0:DEC, 0:2 * CHUNK].rearrange("p (h i) -> p h i", h=2)
                        ).then_inc(score_read[l], 1)
                    if l:
                        dve.wait_ge(stored, 16 * LAYER_STORES * l)
                    dve.wait_ge(ds_done[l], 2)
                    dve.tensor_copy(state[:, :, 1, :], ps[6][:, 0:256].rearrange("p (h v) -> p h v", h=PAIRS)
                                    ).then_inc(st_step[l], 1)
                    done = 1
                    for c in range(1, LAST):
                        dve.wait_ge(st_step[l], done)
                        for h in range(PAIRS):
                            at = (c // 2) * 256 + DV * h
                            last = CHUNK * c + CHUNK - 1
                            dve.scalar_tensor_tensor(
                                out=state[:, h, c + 1, :], in0=state[:, h, c, :], scalar=ga[:, h, last:last + 1],
                                in1=ps[6 + c % 2][:, at:at + DV], op0=ALU.mult, op1=ALU.add).then_inc(st_step[l], 1)
                            done += 1
                    dve.wait_ge(ds_done[l], 3)
                    dve.wait_ge(state_landed, 16 * DEPTH * PAIRS)
                    for h in range(PAIRS):
                        dve.scalar_tensor_tensor(
                            out=state[:, h, S_NEW, :], in0=given[:, l, h, :], scalar=ga[:, h, T - 1:T],
                            in1=ps[4][:, DV * h:DV * h + DV], op0=ALU.mult, op1=ALU.add).then_inc(st_step[l], 1)

                def read_o():
                    for h in range(HEADS):
                        dve.wait_ge(o_done[l], h + 1)
                        dve.tensor_copy(og[:, h, :], ps[4 + h][:, 0:T]).then_inc(o_read[l], 1)

                def weigh_o():
                    dve.wait_ge(silu_done[l], 1)
                    for h in range(HEADS):
                        dve.wait_ge(o_sq[l], h + 1)
                        dve.wait_ge(ms_act[l], HEADS + h + 1)
                        dve.scalar_tensor_tensor(out=og[:, h, :], in0=og[:, h, :], scalar=per_column(o_gn, l),
                                                 in1=proj[:, TV + h, :], op0=ALU.mult, op1=ALU.mult
                                                 ).then_inc(og_step[l], 1)
                        dve.wait_ge(og_step[l], 2 * h + 1)
                        dve.tensor_tensor(og[:, h, :], og[:, h, :], proj[:, TG + h, :], ALU.mult
                                          ).then_inc(og_step[l], 1)

                cv = 0

                def conv_step(ins):
                    nonlocal cv
                    cv += 1
                    ins.then_inc(cv_step[l], 1)
                    return cv

                def conv_pads():
                    if l:
                        dve.wait_ge(var_part, 2 * KT)
                    conv_step(dve.memset(u_ext[:, :, 0:CONV_W - 1], 0.0))
                    at = o_cc + l * (CONV_W - 1) * CT
                    conv_step(dve.tensor_copy(
                        u_ext[:, :, SEQ + CONV_W - 1:SEQ + 2 * (CONV_W - 1)],
                        prm[:, at:at + (CONV_W - 1) * CT].rearrange("p (r t) -> p t r", t=CT)))

                def conv_tiles(g):
                    def run():
                        dve.wait_ge(proj_ready[l], TCH[g] + 2)
                        if g == 0:
                            dve.wait_ge(ds_done[l], 3)
                        else:
                            dve.wait_ge(o_done[l], HEADS)
                        for j in range(2):
                            t = 2 * g + j
                            a, b = proj[:, TCC[g] + j, :], proj[:, TCH[g] + j, :]
                            conv_step(dve.tensor_tensor(u_ext[:, t, 2:2 + SEQ], a[:, 0:SEQ], b[:, 0:SEQ], ALU.mult))
                            n = conv_step(dve.tensor_tensor(u_ext[:, t, SEQ + 4:T + 4], a[:, SEQ:T], b[:, SEQ:T],
                                                            ALU.mult))
                            w = o_cw + l * CONV_W * CT + t
                            dve.wait_ge(cv_step[l], n)
                            n = conv_step(dve.tensor_scalar(conv[g][:, j, :], u_ext[:, t, 0:CVW], per_column(w, 0), None,
                                                            ALU.mult))
                            for tap in range(1, CONV_W):
                                dve.wait_ge(cv_step[l], n)
                                n = conv_step(dve.scalar_tensor_tensor(
                                    out=conv[g][:, j, :], in0=u_ext[:, t, tap:tap + CVW], scalar=per_column(w, CT * tap),
                                    in1=conv[g][:, j, :], op0=ALU.mult, op1=ALU.add))
                    return run

                def conv_out(g):
                    def run():
                        dve.wait_ge(cv_step[l], cv)
                        dve.wait_ge(proj_ready[l], TCB[g] + 2)
                        for j in range(2):
                            c = proj[:, TCB[g] + j, :]
                            conv_step(dve.tensor_tensor(c[:, 0:SEQ], c[:, 0:SEQ], conv[g][:, j, 0:SEQ], ALU.mult))
                            dve.tensor_tensor(c[:, SEQ:T], c[:, SEQ:T], conv[g][:, j, SEQ + 2:CVW], ALU.mult
                                              ).then_inc(y_conv[l], 1)
                    return run

                def rest_y(places):
                    def run():
                        for j in places:
                            k = Y_ORDER[j]
                            dve.wait_ge(yh_ready[l], j + 1)
                            dve.tensor_tensor(y_lo(k), og_tile(k), y_hi(k).bitcast(F32), ALU.subtract
                                              ).then_inc(yl_ready[l], 1)
                    return run

                hooks = {1: [absolute], 2: [log_gates], 3: [gated_qk], 4: [kd, conv_pads], 5: [read_kd],
                         6: [mask_scores], 7: [state_chain], 8: [read_o, conv_tiles(0)], 9: [conv_tiles(1)],
                         10: [weigh_o, rest_y(range(4)), conv_out(0), rest_y(range(4, 6))],
                         11: [conv_out(1), rest_y(range(6, KT))]}
                for u in range(12):
                    if u < 11:
                        rest_unit(U_IN[l] + u + AHEAD)
                    for hook in hooks.get(u, []):
                        hook()
                rest_unit(U_IN[l] + 11 + AHEAD)
                dve.tensor_copy(rows[:, 0, :, :], u_ext[:, :, SEQ:SEQ + 2].rearrange("p t r -> p r t"))
                dve.tensor_copy(rows[:, 1, :, :], u_ext[:, :, T + 2:T + 4].rearrange("p t r -> p r t")
                                ).then_inc(rows_ready[l], 1)
                for u in range(UNITS_OUT):
                    n = U_OUT[l] + u
                    rest_unit(n + AHEAD)
                    for half in range(2):
                        m = 2 * u + half
                        if half:
                            dve.wait_ge(unit_used, n + 1)
                        else:
                            dve.wait_ge(tile_done, TD_OUT[l] + u + 1)
                        dve.scalar_tensor_tensor(out=x[:, m, :], in0=x[:, m, :], scalar=ALPHA, in1=ps[m % 4][:, 0:T],
                                                 op0=ALU.mult, op1=ALU.add).then_inc(r_ready[l], 1)
                        dve.wait_ge(r_ready[l], m + 1)
                        sums = (SUMS[1] if l else 0) + m
                        if m:
                            dve.wait_ge(sum_step, sums)
                            dve.tensor_tensor(rstd[:], rstd[:], x[:, m, :], ALU.add).then_inc(sum_step, 1)
                        else:
                            dve.tensor_copy(rstd[:], x[:, m, :]).then_inc(sum_step, 1)
                dve.wait_ge(r_ready[l], KT)
                norm(2 * l, o_mix_g, o_mix_b, l == 0, clear if l else None)

            def dense_mixer():
                with dve.Fori(0, FC) as c:
                    for j in range(PER_CHUNK):
                        n, q = U_FFN + j, j // 2
                        rest_unit(n + AHEAD, c, PER_CHUNK)
                        if j in (1, 3):
                            dve.wait_ge(d_hl, upto(2 * q, c, 4))
                            for half in range(2):
                                dve.wait_ge(d_silu, upto(2 * q + half + 1, c, 4))
                                if half:
                                    dve.wait_ge(unit_used, upto(n + 1, c, PER_CHUNK))
                                else:
                                    dve.wait_ge(tile_done, upto(TD_FFN + j + 1, c, TD_CHUNK))
                                dve.tensor_tensor(hid[:, half, :], silu_g[:, half, :], ps[2 + half][:, 0:T], ALU.mult
                                                  ).then_inc(d_hid, 1)
                            for half in range(2):
                                dve.wait_ge(d_hh, upto(2 * q + half + 1, c, 4))
                                dve.tensor_tensor(hl[:, 2 * q + half, :], hid[:, half, :],
                                                  hh[:, 2 * q + half, :].bitcast(F32), ALU.subtract).then_inc(d_hl, 1)
                        elif j >= 4:
                            for m in range(4):
                                if j == 4 or m == 3:
                                    dve.wait_ge(unit_used, upto(n + 1, c, PER_CHUNK))
                                else:
                                    dve.wait_ge(tile_done, upto(TD_FFN + 4 + m + 1, c, TD_CHUNK))
                                k = 4 * (j - 4) + m
                                dve.wait_ge(x_ready, KT + k + 1)
                                dve.wait_ge(d_added, upto(k + 1, c, 8))
                                if k < KT // 2:
                                    dve.wait_ge(sum_step, upto(SUMS[0] - HALF_SUM + max(k, 1), c, HALF_SUM))
                                dve.tensor_tensor(x[:, k, :], x[:, k, :], ps[m if j == 5 else 4 + m][:, 0:T], ALU.add
                                                  ).then_inc(d_added, 1)
                dve.wait_ge(d_added, 8 * (FC + 1))
                norm(1, o_ffn_g, o_ffn_b, True)

            def clear():
                dve.wait_ge(unit_used, U_OUT[1] + UNITS_OUT)
                dve.memset(xt_hi[TOK[2]:P, 2, :].bitcast(F32), 0.0)
                dve.memset(xt_lo[TOK[2]:P, 2, :].bitcast(F32), 0.0)
                dve.memset(g_col[:], 0.0)
                dve.memset(pickT[:].bitcast(F32), 0.0)
                dve.memset(ys_hi[:].bitcast(F32), 0.0)
                dve.memset(ys_lo[:].bitcast(F32), 0.0).then_inc(ys_lo_ready, 2)

            def router():
                n = 0

                def xt_rest(first, end):
                    for m in range(first, end):
                        j = XT_ORDER[m]
                        t, half = j // 2, j % 2
                        dve.wait_ge(xth_ready, m + 1)
                        cols = slice(512 * half, 512 * half + 512)
                        dve.tensor_tensor(xt_lo[0:TOK[t], t, cols], ps[2 + j][0:TOK[t], :],
                                          xt_hi[0:TOK[t], t, cols].bitcast(F32), ALU.subtract).then_inc(xtl_ready, 1)

                def read_gather(g):
                    dve.wait_ge(job_done, g + 1)
                    dve.tensor_copy(xg[:, 2 * g:2 * g + 2, :, :].rearrange("p k n s -> p (k n s)"), ps[6 + g % 2][:]
                                    ).then_inc(job_read, 1)

                def step(ins):
                    nonlocal n
                    n += 1
                    ins.then_inc(rt_step, 1)
                    dve.wait_ge(rt_step, n)
                    return n

                step(dve.memset(lg[:], 0.0))
                dve.wait_ge(lg_done, 1)
                for t in range(TT):
                    step(dve.tensor_copy(lg[0:TOK[t], t, :], ps[t][0:TOK[t], 0:E]))
                assert n == RT_LOGITS
                full = [P, TT, E, E]
                mine = lg[:].unsqueeze(3).to_broadcast(full)
                other = lg[:].unsqueeze(2).to_broadcast(full)
                step(dve.tensor_tensor(cmp_gt[:], other, mine, ALU.is_gt))
                step(dve.tensor_tensor(cmp_eq[:], other, mine, ALU.is_equal))
                step(dve.tensor_tensor(cmp_eq[:].rearrange("p t e f -> p t (e f)"),
                                       cmp_eq[:].rearrange("p t e f -> p t (e f)"),
                                       lower_e[:].rearrange("p e f -> p (e f)").unsqueeze(1).to_broadcast([P, TT, E * E]),
                                       ALU.mult))
                step(dve.tensor_tensor(cmp_gt[:], cmp_gt[:], cmp_eq[:], ALU.add))
                step(dve.tensor_reduce(rank[:], cmp_gt[:], AXX, ALU.add))
                step(dve.tensor_scalar(sel1[:], rank[:], 0.0, None, ALU.is_equal))
                step(dve.tensor_scalar(sel2[:], rank[:], 1.0, None, ALU.is_equal))
                step(dve.memset(sel1[TOK[2]:P, 2, :], 0.0))
                step(dve.memset(sel2[TOK[2]:P, 2, :], 0.0))
                step(dve.tensor_tensor(sel[:], sel1[:], sel2[:], ALU.add))
                assert n == RT_SEL
                for m, s in enumerate((sel1, sel2)):
                    step(dve.tensor_tensor(tmp_e[:], s[:], lg[:], ALU.mult))
                    step(dve.tensor_reduce(top[:, m, :], tmp_e[:], AXX, ALU.add))
                step(dve.tensor_tensor(top[:, 2, :], top[:, 1, :], top[:, 0, :], ALU.subtract))
                assert n == RT_DIFF
                xt_rest(0, 4)
                dve.wait_ge(rt_exp, 1)
                step(dve.tensor_scalar(gat[:, 1, :], top[:, 3, :], 1.0, None, ALU.add))
                step(dve.reciprocal(gat[:, 0, :], gat[:, 1, :]))
                step(dve.tensor_tensor(gat[:, 1, :], top[:, 3, :], gat[:, 0, :], ALU.mult))
                step(dve.tensor_tensor(comb[:], sel1[:], gat[:, 0, :].unsqueeze(2).to_broadcast([P, TT, E]), ALU.mult))
                step(dve.tensor_tensor(tmp_e[:], sel2[:], gat[:, 1, :].unsqueeze(2).to_broadcast([P, TT, E]), ALU.mult))
                step(dve.tensor_tensor(comb[:], comb[:], tmp_e[:], ALU.add))
                dve.wait_ge(pos_done, 1)
                step(dve.scalar_tensor_tensor(out=qpos[:], in0=ps[1][:, 0:TT * E].rearrange("p (t e) -> p t e", e=E),
                                              scalar=1.0, in1=sel[:], op0=ALU.add, op1=ALU.mult))
                step(dve.tensor_copy(q_tab[:, :, 0:E], qpos[:]))
                step(dve.tensor_copy(g_tab[:, :, 0:E], comb[:]))
                make_pick(0)
                xt_rest(4, 2 * TT)
                flat_over = over[:].rearrange("p j e -> p (j e)")
                shape = [P, MORE + 1, 2 * E]
                wide4 = wide[:].rearrange("p (t s) n -> p t s n", t=TT)

                def overfull():
                    for j in range(2):
                        step(dve.tensor_scalar(over[:, j, :], ps[1][:, TT * E:TT * E + E], float(P * (j + 1)), None,
                                               ALU.is_gt))
                    step(dve.tensor_tensor_scan(over_n[:], ones[:, 0:2 * E], flat_over, 0.0, ALU.mult, ALU.add))
                    step(dve.tensor_scalar(over_i[:], over_n[:], float(E - 1), None, ALU.add))
                    step(dve.tensor_tensor(slot_of[:], more_no[:], over_i[:].unsqueeze(1).to_broadcast(shape),
                                           ALU.is_equal))
                    step(dve.tensor_tensor(slot_of[:], slot_of[:], flat_over.unsqueeze(1).to_broadcast(shape), ALU.mult))

                def item_experts():
                    step(dve.tensor_tensor(wide4[:, 0], slot_of[:],
                                           exp_no[:].rearrange("p j e -> p (j e)").unsqueeze(1).to_broadcast(shape),
                                           ALU.mult))
                    step(dve.tensor_reduce(ctl_f[:, 0:MORE + 1], wide4[:, 0], AXX, ALU.add))
                    step(dve.tensor_scalar(ctl_f[:, MORE + 1:MORE + 2], over_n[:, 2 * E - 1:2 * E], float(E), None,
                                           ALU.add))
                    dve.tensor_copy(ctl[0:1, 0:MORE + 2], ctl_f[0:1, 0:MORE + 2]).then_inc(ctl_ready, 1)

                def shifted():
                    for j in range(2):
                        step(dve.tensor_scalar(qsh[:, :, E * j:E * j + E], qpos[:], float(-P * (j + 1)), None, ALU.add))
                        step(dve.tensor_copy(csh[:, :, E * j:E * j + E], comb[:]))

                def table(tab, of):
                    for t in range(TT):
                        step(dve.tensor_tensor(wide4[:, t], slot_of[:], of[:, t, :].unsqueeze(1).to_broadcast(shape),
                                               ALU.mult))
                    step(dve.tensor_reduce(tab[:, :, E:SLOTS], wide4, AXX, ALU.add))

                overfull()
                item_experts()
                read_gather(0)
                read_gather(1)
                shifted()
                read_gather(2)
                read_gather(3)
                table(q_tab, qsh)
                table(g_tab, csh)

            def make_pick(i):
                at = slice(i, i + 1) if isinstance(i, int) else bass.ds(i, 1)
                for t in range(TT):
                    dve.tensor_scalar(pick[:, t, :], slot_no[:], q_tab[:, t, at], None, ALU.is_equal)
                dve.tensor_copy(g_col[:].unsqueeze(2), g_tab[:, :, at]).then_inc(pick_ready, 1)

            def experts(items):
                with dve.Fori(0, items) as i:
                    unit, job, chunk = 0, GATHERS, 0
                    for part, c, half in ITEM:
                        if part in ("gate", "up", "down"):
                            n = U_MOE + unit
                            unit += 1
                            rest_unit(n + AHEAD, i, PER_ITEM)
                            if part == "up" and half:
                                dve.wait_ge(unit_used, upto(n + 1, i, PER_ITEM))
                                dve.wait_ge(m_silu, upto(c + 1, i, FC))
                                dve.tensor_tensor(hm[:, c % 2, :], sg[:, c % 2, :], ps[2 * (c % 2) + 1][:], ALU.mult
                                                  ).then_inc(m_hid, 1)
                            continue
                        bank = ps[6 + job % 2]
                        dve.wait_ge(job_done, upto(job + 1, i, PER_JOBS))
                        if part == "T":
                            chunk += 1
                            dve.wait_ge(hT_hi_ready, upto(chunk, i, FC))
                            dve.tensor_tensor(hT_lo[:, :, :].rearrange("p f s -> p (f s)"), bank[:],
                                              hT_hi[:, :, :].rearrange("p f s -> p (f s)").bitcast(F32), ALU.subtract
                                              ).then_inc(job_read, 1)
                        elif part == "S":
                            if c == 0:
                                dve.wait_ge(x_scaled, 1)
                            dve.wait_ge(job_read, upto(job, i, PER_JOBS))
                            dve.tensor_tensor(x[:, c, :], x[:, c, :], bank[:, 0:T], ALU.add).then_inc(job_read, 1)
                        elif part == "GT":
                            dve.wait_ge(ys_ready, upto(0, i, 2))
                            dve.tensor_copy(pickT[:], bank[:, 0:T])
                            dve.tensor_copy(g_slot[:, 0:1], bank[:, T:T + 1]).then_inc(job_read, 1)
                            make_pick(dve.snap(i + 1))
                        else:
                            dve.tensor_copy(xg[:, 2 * c:2 * c + 2, :, :].rearrange("p k n s -> p (k n s)"), bank[:]
                                            ).then_inc(job_read, 1)
                        job += 1
                    for d in range(2):
                        dve.wait_ge(ys_hi_ready, upto(d + 1, i, 2))
                        cols = slice(512 * d, 512 * d + 512)
                        dve.tensor_tensor(ys_lo[:, cols], ys[:, cols], ys_hi[:, cols].bitcast(F32), ALU.subtract
                                          ).then_inc(ys_lo_ready, 1)
                dve.wait_ge(job_read, items * PER_JOBS + GATHERS)
                for k in range(KT):
                    dve.wait_ge(job_done, items * PER_JOBS + (GATHERS + k + 1))
                    dve.tensor_tensor(x[:, k, :], x[:, k, :], ps[TAIL_BANKS[k % 4]][:, 0:T], ALU.add
                                      ).then_inc(job_read, 1)
                dve.wait_ge(job_read, items * PER_JOBS + (GATHERS + KT))
                norm(3, o_ffn_g, o_ffn_b, False)

            mixer(0)
            dense_mixer()
            mixer(1)
            router()
            dve.wait_ge(ctl_ready, 1)
            items = dve.value_load(ctl[0:1, MORE + 1:MORE + 2], min_val=E, max_val=E + MORE)
            experts(items)
            for t in range(TT):
                dve.wait_ge(y_turned, TT + t + 1)
                dve.tensor_copy(y_tok[0:TOK[t], t, 512:1024], ps[1 + 2 * (t % 2) if t < 2 else 7][0:TOK[t], :]
                                ).then_inc(y_ready_v, 1)


_INS = ["x_prompt", "x_sample", "cache_conv", "state_gla", "ln_mix_g", "ln_mix_b", "w_in", "w_alpha2", "b_alpha",
        "conv_w", "gla_norm_g", "w_out", "ln_ffn_g", "ln_ffn_b", "ffn_w_gate", "ffn_w_up", "ffn_w_down",
        "moe_router", "moe_w_gate", "moe_w_up", "moe_w_down"]


def kernel(**inputs):
    import numpy as np
    import concourse.bacc as bacc
    from concourse.bass_utils import run_bass_kernel_spmd

    nc = bacc.Bacc("TRN2", target_bir_lowering=False, num_devices=1)
    arrays, args = {}, []
    for name in _INS:
        a = np.ascontiguousarray(inputs[name])
        arrays[f"in_{name}"] = a
        args.append(nc.dram_tensor(f"in_{name}", a.shape, mybir.dt.from_np(a.dtype), kind="ExternalInput").ap())
    depth, _, heads, dk, dv = inputs["state_gla"].shape
    _, _, rows, conv = inputs["cache_conv"].shape
    shapes = [inputs["x_prompt"].shape, inputs["x_sample"].shape,
              (depth, inputs["x_prompt"].shape[0], heads, dk, dv), (depth, inputs["x_prompt"].shape[0], rows, conv),
              inputs["state_gla"].shape, inputs["cache_conv"].shape]
    for i, shape in enumerate(shapes):
        args.append(nc.dram_tensor(f"out_{i}", shape, F32, kind="ExternalOutput").ap())
    hybrid_stream_step(nc, *args)
    r = run_bass_kernel_spmd(nc, [arrays], core_ids=[0])
    return tuple(r.results[0][f"out_{i}"] for i in range(len(shapes)))
```
